# Optimizing a Trainium2 kernel written in Bass

```python
import math
import jax, jax.numpy as jnp
from jax import lax
import numpy as np

D_MODEL = 1024
BATCH = 1
SEQ = 512
DEPTH = 1

RET_HEADS = 4
RET_QK_DIM = 64
RET_V_DIM = 128
RET_WIDTH = RET_HEADS * RET_V_DIM
RET_CHUNK = 128
ROPE_BASE = 10000.0
CONV_CH = 512
CONV_K = 31
IN_SPLITS = (RET_HEADS * RET_QK_DIM, RET_HEADS * RET_QK_DIM, RET_WIDTH, RET_WIDTH,
             CONV_CH, CONV_CH, D_MODEL, D_MODEL)
IN_COLS = sum(IN_SPLITS)
PEER_HEADS = 8
PEER_QDIM = 256
PEER_HALF = PEER_QDIM // 2
N_KEYS = 128
N_EXPERTS = N_KEYS * N_KEYS
PEER_TOPK = 16
TOKEN_BLOCK = 128

RMS_EPS = 1e-6
LN_EPS = 1e-5

kernel_name = "hybrid_retention_conformer_peer"

def rms_norm(x, g):
    xf = x.astype(jnp.float32)
    y = xf * lax.rsqrt(jnp.mean(xf * xf, axis=-1, keepdims=True) + RMS_EPS)
    return (y * g.astype(jnp.float32)).astype(x.dtype)

def layer_norm(x, g, b):
    xf = x.astype(jnp.float32)
    mu = jnp.mean(xf, axis=-1, keepdims=True)
    var = jnp.mean(jnp.square(xf - mu), axis=-1, keepdims=True)
    y = (xf - mu) * lax.rsqrt(var + LN_EPS)
    return (y * g.astype(jnp.float32) + b.astype(jnp.float32)).astype(x.dtype)

def rotary(t):
    s, d = t.shape[1], t.shape[-1]
    half = d // 2
    inv = 1.0 / (ROPE_BASE ** (jnp.arange(half, dtype=jnp.float32) / half))
    ang = jnp.arange(s, dtype=jnp.float32)[:, None] * inv[None, :]
    cos = jnp.cos(ang)[None, :, None, :]
    sin = jnp.sin(ang)[None, :, None, :]
    tf = t.astype(jnp.float32)
    t1, t2 = tf[..., :half], tf[..., half:]
    return jnp.concatenate([t1 * cos - t2 * sin, t1 * sin + t2 * cos], axis=-1)

def chunkwise_retention(q, k, v):
    bsz, s, h, dk = q.shape
    dv = v.shape[-1]
    n_chunks = s // RET_CHUNK
    c = RET_CHUNK
    log_gamma = jnp.log1p(-(2.0 ** (-5.0 - jnp.arange(h, dtype=jnp.float32))))
    n_idx = jnp.arange(c, dtype=jnp.float32)
    diff = n_idx[:, None] - n_idx[None, :]
    intra = jnp.where(diff[None] >= 0, jnp.exp(log_gamma[:, None, None] * jnp.maximum(diff, 0.0)[None]), 0.0)
    q_decay = jnp.exp(log_gamma[:, None] * (n_idx + 1.0)[None])
    k_decay = jnp.exp(log_gamma[:, None] * (c - 1.0 - n_idx)[None])
    chunk_decay = jnp.exp(log_gamma * c)

    def to_chunks(t):
        return t.reshape(bsz, n_chunks, c, h, t.shape[-1]).transpose(1, 0, 3, 2, 4)

    qc, kc, vc = to_chunks(q), to_chunks(k), to_chunks(v)

    def step(state, inp):
        qi, ki, vi = inp
        scores = jnp.einsum('bhnd,bhmd->bhnm', qi, ki) * intra[None]
        inner = jnp.einsum('bhnm,bhme->bhne', scores, vi)
        cross = jnp.einsum('bhnd,bhde->bhne', qi, state) * q_decay[None, :, :, None]
        new_state = state * chunk_decay[None, :, None, None] + jnp.einsum(
            'bhmd,bhme->bhde', ki * k_decay[None, :, :, None], vi)
        return new_state, inner + cross

    state0 = jnp.zeros((bsz, h, dk, dv), jnp.float32)
    _, out = lax.scan(step, state0, (qc, kc, vc))
    return out.transpose(1, 0, 3, 2, 4).reshape(bsz, s, h, dv)

def retention_branch(q, k, v, g, gn_g, w_proj):
    bsz, s, _ = q.shape
    dt = q.dtype
    q = rotary(q.reshape(bsz, s, RET_HEADS, RET_QK_DIM))
    k = rotary(k.reshape(bsz, s, RET_HEADS, RET_QK_DIM)) * (RET_QK_DIM ** -0.5)
    v = v.reshape(bsz, s, RET_HEADS, RET_V_DIM).astype(jnp.float32)
    o = chunkwise_retention(q, k, v)
    mu = jnp.mean(o, axis=-1, keepdims=True)
    var = jnp.mean(jnp.square(o - mu), axis=-1, keepdims=True)
    o = (o - mu) * lax.rsqrt(var + LN_EPS) * gn_g.astype(jnp.float32)[None, None]
    o = o.reshape(bsz, s, RET_WIDTH).astype(dt)
    return (jax.nn.silu(g) * o) @ w_proj

def conv_branch(u_val, u_gate, dw_w, dw_b, ln_g, ln_b, w_proj, b_proj):
    c = u_val * jax.nn.sigmoid(u_gate)
    c = lax.conv_general_dilated(
        c, dw_w[:, None, :].astype(c.dtype), window_strides=(1,),
        padding=[(CONV_K - 1, 0)], dimension_numbers=('NWC', 'WIO', 'NWC'),
        feature_group_count=CONV_CH) + dw_b
    c = jax.nn.silu(layer_norm(c, ln_g, ln_b))
    return c @ w_proj + b_proj

def peer_ffn(hn, w_query, sub_keys, u_tab, v_tab):
    bsz, s, d = hn.shape
    t = bsz * s
    hf = hn.reshape(t, d)
    q = (hf @ w_query).reshape(t, PEER_HEADS, 2, PEER_HALF)
    scores = jnp.einsum('thpd,hpnd->thpn', q, sub_keys).astype(jnp.float32)
    s1, i1 = lax.top_k(scores[:, :, 0], PEER_TOPK)
    s2, i2 = lax.top_k(scores[:, :, 1], PEER_TOPK)
    cand = (s1[..., :, None] + s2[..., None, :]).reshape(t, PEER_HEADS, PEER_TOPK * PEER_TOPK)
    best, pos = lax.top_k(cand, PEER_TOPK)
    e1 = jnp.take_along_axis(i1, pos // PEER_TOPK, axis=-1)
    e2 = jnp.take_along_axis(i2, pos % PEER_TOPK, axis=-1)
    experts = (e1 * N_KEYS + e2).reshape(t, PEER_HEADS * PEER_TOPK)
    gates = jax.nn.softmax(best, axis=-1).reshape(t, PEER_HEADS * PEER_TOPK).astype(hn.dtype)

    nb = t // TOKEN_BLOCK
    kk = PEER_HEADS * PEER_TOPK

    def apply_block(inp):
        hb, eb, gb = inp
        u = u_tab[eb]
        a = jax.nn.gelu(jnp.einsum('td,tkd->tk', hb, u), approximate=False) * gb
        return jnp.einsum('tk,tkd->td', a, v_tab[eb])

    out = lax.map(apply_block, (hf.reshape(nb, TOKEN_BLOCK, d),
                                experts.reshape(nb, TOKEN_BLOCK, kk),
                                gates.reshape(nb, TOKEN_BLOCK, kk)))
    return out.reshape(bsz, s, d)

def setup_inputs(seed: int = 0) -> dict:
    key = jax.random.key(seed)
    ks = jax.random.split(key, 20)
    nrm = jax.random.normal
    f32 = jnp.float32
    return {
        "x": nrm(ks[0], (BATCH, SEQ, D_MODEL), f32),
        "rms_mix_g": 1.0 + 0.02 * nrm(ks[1], (DEPTH, D_MODEL), f32),
        "w_in": nrm(ks[2], (DEPTH, D_MODEL, IN_COLS), f32) * D_MODEL ** -0.5,
        "ret_gn_g": 1.0 + 0.02 * nrm(ks[3], (DEPTH, RET_HEADS, RET_V_DIM), f32),
        "conv_dw_w": nrm(ks[4], (DEPTH, CONV_K, CONV_CH), f32) * CONV_K ** -0.5,
        "conv_dw_b": 0.02 * nrm(ks[5], (DEPTH, CONV_CH), f32),
        "conv_ln_g": 1.0 + 0.02 * nrm(ks[6], (DEPTH, CONV_CH), f32),
        "conv_ln_b": 0.02 * nrm(ks[7], (DEPTH, CONV_CH), f32),
        "w_ret_proj": nrm(ks[8], (DEPTH, RET_WIDTH, D_MODEL), f32) * RET_WIDTH ** -0.5,
        "w_conv_proj": nrm(ks[9], (DEPTH, CONV_CH, D_MODEL), f32) * CONV_CH ** -0.5,
        "b_conv_proj": 0.02 * nrm(ks[10], (DEPTH, D_MODEL), f32),
        "w_out": nrm(ks[11], (DEPTH, D_MODEL, D_MODEL), f32) * D_MODEL ** -0.5,
        "rms_ffn_g": 1.0 + 0.02 * nrm(ks[12], (DEPTH, D_MODEL), f32),
        "w_query": nrm(ks[13], (DEPTH, D_MODEL, PEER_HEADS * PEER_QDIM), f32) * D_MODEL ** -0.5,
        "peer_sub_keys": nrm(ks[14], (DEPTH, PEER_HEADS, 2, N_KEYS, PEER_HALF), f32) * PEER_HALF ** -0.5,
        "peer_u": nrm(ks[15], (DEPTH, N_EXPERTS, D_MODEL), f32) * D_MODEL ** -0.5,
        "peer_v": nrm(ks[16], (DEPTH, N_EXPERTS, D_MODEL), f32) * 0.5,
        "rms_final_g": 1.0 + 0.02 * nrm(ks[17], (D_MODEL,), f32),
    }

def reference(x, rms_mix_g, w_in, ret_gn_g, conv_dw_w, conv_dw_b, conv_ln_g, conv_ln_b,
              w_ret_proj, w_conv_proj, b_conv_proj, w_out, rms_ffn_g, w_query,
              peer_sub_keys, peer_u, peer_v, rms_final_g):
    split_points = list(np.cumsum(IN_SPLITS)[:-1])
    for l in range(DEPTH):
        h = rms_norm(x, rms_mix_g[l])
        proj = h @ w_in[l]
        q, k, v, g_ret, u_val, u_gate, gate_a, gate_b = jnp.split(proj, split_points, axis=-1)
        a = retention_branch(q, k, v, g_ret, ret_gn_g[l], w_ret_proj[l])
        b = conv_branch(u_val, u_gate, conv_dw_w[l], conv_dw_b[l], conv_ln_g[l], conv_ln_b[l],
                        w_conv_proj[l], b_conv_proj[l])
        mixed = jax.nn.sigmoid(gate_a) * a + jax.nn.sigmoid(gate_b) * b
        x = x + mixed @ w_out[l]
        hn = rms_norm(x, rms_ffn_g[l])
        x = x + peer_ffn(hn, w_query[l], peer_sub_keys[l], peer_u[l], peer_v[l])
    return rms_norm(x, rms_final_g)


_drawn_inputs = setup_inputs


def setup_inputs(seed=0):
    import zlib

    import numpy as np

    out = dict(_drawn_inputs(seed))
    spreads = {}
    factors = {}
    for name, (base, spread) in spreads.items():
        noise = np.random.default_rng([zlib.crc32(name.encode()), seed]).standard_normal(out[name].shape)
        drawn = base * np.exp(spread * noise) if base else spread * noise
        out[name] = __import__('jax').numpy.asarray(drawn.astype(out[name].dtype))
    for name, factor in factors.items():
        out[name] = (out[name] * factor).astype(out[name].dtype)
    return out
```

```python
from contextlib import ExitStack

import concourse.bass as bass
from concourse import mybir

P = 128
T = 512
TT = T // P
D = 1024
DC = D // P
H = 4
CH = 4
TAPS = 31
HP = 16
HEADS = 8
TOPK = 16
NKEY = 128

F32 = mybir.dt.float32
F32R = mybir.dt.float32r
U32 = mybir.dt.uint32
ALU = mybir.AluOpType
ACT = mybir.ActivationFunctionType
AX = mybir.AxisListType
NEG = -3.0e38
RMS_EPS, LN_EPS = 1e-6, 1e-5

UVAL, UGATE, QK, VV, GRET = 0, 1, 2, 3, 4
GATE_A, GATE_B, PROJ, WOUT, QUERY, EXPERTS = 5, 7, 9, 11, 13, 17
FRONT = 4 * EXPERTS
N_U = NKEY
GROUPS = N_U // 4
AHEAD = 4
ROWS = (QK, VV, WOUT, WOUT + 1)


SIDE = [("XT", c) for c in range(DC)] + [("QKT", b) for b in range(4)]
for _c in range(TT):
    SIDE += [("S", 0)] if _c == 0 else []
    SIDE += [("O", _c)]
    SIDE += [("ST", _c), ("S", _c + 1)] if _c < TT - 1 else []
SIDE += [("YT", h) for h in range(H)] + [("MU", 0), ("VAR", 0)]
SIDE += [("PB", i) for i in range(DC)] + [("HT", c) for c in range(DC)]
SIDE += [("SC", i) for i in range(HP)] + [("ET", t) for t in range(TT)]
SIDE_AT = {name: m for m, name in enumerate(SIDE)}
GATE0 = len(SIDE)
BATCH = 4
NBATCH = T // BATCH
TBLK = 32
PER_BLK = TBLK // BATCH
NBLK = T // TBLK
OUT0 = GATE0 + NBATCH
LAST = GROUPS - AHEAD

RECTS = [(0, 1, 16), (1, 2, 8), (2, 4, 5), (4, 8, 3), (8, 16, 1)]
NCAND = sum((b - a) * w for a, b, w in RECTS)

CONSTS = [("ident", 128), ("iota", 128), ("ones", 128), ("cos", TT * 64), ("sin", TT * 64), ("mask", H * 128),
          ("qdec", 256), ("kdec", H), ("cdec", 2), ("half", 2)]
PARAMS = [("g_mix", DC), ("g_ffn", DC), ("gn", H), ("ln_g", CH), ("ln_b", CH), ("dwb", CH), ("bproj", DC),
          ("dww", CH * TAPS)]


def offsets(table):
    at, out = 0, {}
    for name, n in table:
        out[name] = (at, n)
        at += n
    return out, at


N_SMALL = 152
CONST_AT, N_CONST = offsets(CONSTS)
PARAM_AT, N_PARAM = offsets(PARAMS)


def build(nc, x, wfront, ut, peer_v, keys, consts, params, gfin, out):
    spill = nc.dram_tensor("gates_spill", (P, NBLK, NKEY, TBLK), F32, kind="Internal").ap()
    KB = 1024
    base = (nc.sbuf_base + 31) // 32 * 32

    def at(name, shape, kb, dt=F32):
        return nc.alloc_sbuf_tensor_at(name, shape, dt, offset=base + int(kb * KB))

    res = at("res", [P, TT, D], 0)
    hH = at("hH", [P, DC, T], 16, F32R)
    hL = at("hL", [P, DC, T], 32, F32R)
    wraw = at("wraw", [P, 4, DC, P], 48)
    gfb = at("gfb", [P, D], 48)
    wH = at("wH", [P, 4, DC, P], 64, F32R)
    fjunk = at("fjunk", [P, D], 64)
    wL = at("wL", [P, 4, DC, P], 80, F32R)
    cst = at("cst", [P, N_CONST], 96)
    prm_kb = 96 + (N_CONST + 7) // 8 * 32 / KB
    small_kb = prm_kb + (N_PARAM + 7) // 8 * 32 / KB
    prm = at("prm", [P, N_PARAM], prm_kb)
    small = at("small", [P, N_SMALL], small_kb)
    W = 103 + 25 / 32
    assert small_kb + N_SMALL * 4 / KB <= W
    qkraw = at("qkraw", [P, TT, 512], W + 0)
    qkrot = at("qkrot", [P, TT, 512], W + 8)
    sa = at("sa", [P, DC, T], W + 0)
    vt = at("vt", [P, TT, 512], W + 16)
    gs = at("gs", [P, H, T], W + 24)
    yL = at("yL", [P, DC, T], W + 16, F32R)
    kT = at("kT", [P, 2, T], W + 32)
    qz = at("qz", [P, H, T], W + 36)
    kd = at("kd", [P, TT, 256], W + 44)
    sb = at("sb", [P, DC, T], W + 32)
    rtmp = at("rtmp", [P, 4, 256], W + 48)
    scm = at("scm", [P, 2, 512], W + 48)
    stat = at("stat", [P, 2, 2, 128], W + 52)
    rsd = at("rsd", [P, T], W + 50)
    val = at("val", [P, CH, T], W + 54)
    qdz = at("qdz", [P, H, T], W + 54)
    sqc = at("sqc", [P, CH, T], W + 54)
    tb = at("tb", [P, 2, T], W + 54)
    cpad = at("cpad", [P, CH, T + TAPS - 1], W + 62)
    sg = at("sg", [P, CH, T], W + 71)
    cacc = at("cacc", [P, CH, T], W + 71)
    yH = at("yH", [P, DC, T], W + 79, F32R)
    osb = at("osb", [P, TT, 512], W + 95)
    xn = at("xn", [P, TT, D], W + 16)
    hraw = at("hraw", [P, DC, T], W + 32)
    junk = at("junk", [P, D], W + 48)
    keyT = at("keyT", [P, HP, NKEY], W + 0)
    e1f = at("e1f", [P, TT, P], W + 0)
    e2f = at("e2f", [P, TT, P], W + 2)
    gtf = at("gtf", [P, TT, P], W + 4)
    eT = at("eT", [P, 3, T], W + 8)
    s16 = at("s16", [P, 2, 2, TT, TOPK], W + 14)
    ix = at("ix", [P, 2, 2, TT, TOPK], W + 15, U32)
    qT = at("qT", [P, HP, T], W + 16)
    dec = at("dec", [P, 4, TT * P], W + 24)
    stage = at("stage", [P, 2, NKEY, TBLK], W + 16)
    sc = at("sc", [P, 4, 2, TT, NKEY], W + 48)
    hot = at("hot", [P, 2, HEADS, TOPK, TOPK], W + 48)
    cand = at("cand", [P, 2, TT, NCAND], W + 64)
    b16 = at("b16", [P, 2, TT, TOPK], W + 65.75)
    p16 = at("p16", [P, 2, TT, TOPK], W + 66.25, U32)
    oh = at("oh", [P, 4, 2, BATCH, P], W + 48)
    gblk = at("gblk", [P, TBLK], W + 6)
    i1f = at("i1f", [P, TT, HEADS, TOPK], W + 16)
    i2f = at("i2f", [P, TT, HEADS, TOPK], W + 18)
    best = at("best", [P, TT, HEADS, TOPK], W + 20)
    pos = at("pos", [P, TT, HEADS, TOPK], W + 22)
    irank = at("irank", [P, TT * P], W + 22)
    jrank = at("jrank", [P, TT * P], W + 6)
    vraw = at("vraw", [P, 4, D], W + 0)
    vH = at("vH", [P, 4, D], W + 16, F32R)
    vL = at("vL", [P, 4, D], W + 32, F32R)
    aH = at("aH", [P, 4, T], W + 48, F32R)
    aL = at("aL", [P, 4, T], W + 56, F32R)
    dg = at("dg", [P, NBLK, 4, TBLK], W + 64)
    gel = at("gel", [P, 4, 4, T], W + 72)

    def C(name):
        a, n = CONST_AT[name]
        return cst[:, a:a + n]

    def PR(name, i):
        a, _ = PARAM_AT[name]
        return prm[:, a + i:a + i + 1]

    def bc(ap, axis, n):
        ap = ap.unsqueeze(axis)
        shape = list(ap.shape)
        shape[axis] = n
        return ap.to_broadcast(shape)

    def f(ap):
        return ap.bitcast(F32)

    ident, iota, ones = C("ident"), C("iota"), C("ones")
    cosv = C("cos").rearrange("p (t s i) -> p t s i", t=TT, s=2)
    sinv = C("sin").rearrange("p (t s i) -> p t s i", t=TT, s=2)
    ssq, rst = small[:, 0:4], small[:, 4:8]
    bst = small[:, 8:104].rearrange("p (n s) -> p n s", s=6)
    mv = small[:, 104:136].rearrange("p (n s) -> p n s", s=2)
    grs = small[:, 136:152]
    zs = small[:, 8:40]

    two_sets = ((vH, vL, aH, aL), (wH[:, :, :, :].rearrange("p j c n -> p j (c n)"), wL[:, :, :, :].rearrange("p j c n -> p j (c n)"),
                                   hH[:, 0:4, :], hL[:, 0:4, :]))

    def operands(i):
        return two_sets[0 if i is None else (i - LAST + 1) % 2]

    ctx = ExitStack()
    psum = ctx.enter_context(nc.psum_tensor("psum", [P, 8, 512], F32))

    iota_psum = psum[:, 0, 0:P]

    def stream(n):
        return psum[:, n % 4, :]

    def side(m):
        return psum[:, 4 + m % 4, :]

    def sem(name):
        return ctx.enter_context(nc.semaphore(name))

    x_in = [sem(f"x_in{i}") for i in range(TT)]
    cst_in, prm_in, key_in, gfin_in = sem("cst_in"), sem("prm_in"), sem("key_in"), sem("gfin_in")
    w_in = [sem(f"w_in{i}") for i in range(4)]
    v_in = [sem(f"v_in{i}") for i in range(4)]
    d_in = sem("d_in")
    wh_done, wl_done = sem("wh_done"), sem("wl_done")
    vh_done, vl_done = sem("vh_done"), sem("vl_done")
    bank_done = sem("bank_done")
    rows_done = sem("rows_done")
    bank_free = sem("bank_free")
    side_done = sem("side_done")
    side_free = [sem(f"side_free{i}") for i in range(4)]
    sq_done, ms_done, rt_done, xn_done = sem("sq_done"), sem("ms_done"), sem("rt_done"), sem("xn_done")
    hh_done, hl_done = sem("hh_done"), sem("hl_done")
    pad_done, conv_in, conv_step = sem("pad_done"), sem("conv_in"), sem("conv_step")
    rot_done, kd_done, qd_done, state_done = (sem(n) for n in ("rot_done", "kd_done", "qd_done", "state_done"))
    y_done, yh_done, yl_done = sem("y_done"), sem("yh_done"), sem("yl_done")
    cen_done, sqc_done, cn_done, yc_done = sem("cen_done"), sem("sqc_done"), sem("cn_done"), sem("yc_done")
    mix_done = sem("mix_done")
    topk, topk_head = sem("topk"), sem("topk_head")
    exp_in, exp_done, hot_done, hotx_done, pick_done = (sem(n) for n in ("exp_in", "exp_done", "hot_done", "hotx_done", "pick_done"))
    gblk_done, oh_done, ohg_done, iota_done = (sem(n) for n in ("gblk_done", "oh_done", "ohg_done", "iota_done"))
    stored = [sem("stored0"), sem("stored1")]
    a_done, ah_done, al_done = sem("a_done"), sem("ah_done"), sem("al_done")
    fin_done, out_done = sem("fin_done"), sem("out_done")
    dve_step, act_step, pool_step = sem("dve_step"), sem("act_step"), sem("pool_step")

    def bank_ready(n):
        g, j = n // 4, n % 4
        return (rows_done, 3 * ROWS.index(g) + j + 1) if g in ROWS and j < 3 else (bank_done, n + 1)

    def evacuated(m):
        return side_free[m % 4], m // 4 + 1

    def side_at(name, i=0):
        return SIDE_AT[(name, i)]

    passed = {e: sem(f"passed_{e}") for e in ("sp", "dve", "pool")}

    def wait_now(eng, name, s, value):
        eng.wait_ge(s, value)
        eng.sem_inc(passed[name], 1)

    block = ctx.enter_context(nc.Block())

    @block.sync
    def _(sp):
        for tt in range(TT):
            sp.dma_start(res[:, tt, :], x[tt * P:(tt + 1) * P, :]).then_inc(x_in[tt], 16)
        sp.dma_start(cst[:, :], consts).then_inc(cst_in, 16)
        sp.dma_start(prm[:, :], params).then_inc(prm_in, 16)

        def load_w(n, src, count):
            if count is not None:
                sp.wait_ge(wh_done, count)
                wait_now(sp, "sp", wl_done, count)
            sp.dma_start(wraw[:, n % 4, :, :].rearrange("p c n -> p (c n)"), src).then_inc(w_in[n % 4], 16)

        for n in range(FRONT + 4 * AHEAD + 7):
            src = wfront[n] if n < FRONT else ut[n - FRONT]
            load_w(n, src, n - 3 if n >= 4 else None)
            if n == FRONT - 16:
                sp.wait_ge(hl_done, 2 * DC)
                sp.dma_start(keyT[:, :, :].rearrange("p a b -> p (a b)"), keys).then_inc(key_in, 16)

        with sp.Fori(0, NBLK // 2) as b2:
            for s in range(2):
                for k in range(PER_BLK):
                    m = GATE0 + s * PER_BLK + k
                    if k >= PER_BLK - 4:
                        wait_now(sp, "sp", side_free[m % 4], m // 4 + 1 + b2 * (2 * PER_BLK // 4))
                sp.dma_start(spill[:, bass.ds(b2 * 2 + s, 1), :, :].rearrange("p a e t -> p (a e t)"),
                             stage[:, s, :, :].rearrange("p e t -> p (e t)")).then_inc(stored[s], 16)

        def load_v(j, i):
            sp.dma_start(vraw[:, j, :], peer_v[:, bass.ds(i * 4 + j, 1), :].rearrange("p a d -> p (a d)")).then_inc(v_in[j], 16)

        def load_d(i):
            sp.dma_start(dg[:, :, :, :].rearrange("p b e t -> p b (e t)"),
                         spill[:, :, bass.ds(i * 4, 4), :].rearrange("p b e t -> p b (e t)")).then_inc(d_in, 16)

        sp.wait_ge(stored[0], 16 * NBLK // 2)
        sp.wait_ge(stored[1], 16 * NBLK // 2)
        load_d(0)
        for j in range(4):
            load_v(j, 0)
        with sp.Fori(0, GROUPS - AHEAD - 2) as i:
            for j in range(4):
                load_w(j + 3, ut[bass.ds(i * 4 + 4 * AHEAD + j + 7, 1), :, :].rearrange("a p f -> p (a f)"),
                       i * 4 + FRONT + 4 * AHEAD + j + 4)
                sp.wait_ge(vh_done, i * 4 + j + 1)
                wait_now(sp, "sp", vl_done, i * 4 + j + 1)
                load_v(j, i + 1)
            wait_now(sp, "sp", a_done, i * 4 + 4)
            load_d(i + 1)
        for i in range(GROUPS - AHEAD - 2, GROUPS - 1):
            for j in range(4):
                n = 4 * (i + AHEAD) + j + 7
                if n < N_U:
                    load_w(FRONT + n, ut[n], FRONT + n - 3)
                sp.wait_ge(vh_done, 4 * i + j + 1)
                sp.wait_ge(vl_done, 4 * i + j + 1)
                load_v(j, i + 1)
            sp.wait_ge(a_done, 4 * i + 4)
            load_d(i + 1)
        sp.wait_ge(wl_done, FRONT + N_U)
        sp.wait_ge(wh_done, FRONT + N_U)
        sp.dma_start(gfb[:, :], gfin).then_inc(gfin_in, 16)
        for tt in range(TT):
            sp.wait_ge(fin_done, tt + 1)
            sp.dma_start(out[tt * P:(tt + 1) * P, :], res[:, tt, :]).then_inc(out_done, 16)
        sp.wait_ge(out_done, 16 * TT)

    @block.tensor
    def _(pe):
        def three(bank, lhs, rhs, first, last, **kw):
            (lh, ll), (rh, rl) = lhs, rhs
            pe.matmul(bank, lh, rh, start=first, stop=False)
            pe.matmul(bank, lh, rl, start=False, stop=False)
            return pe.matmul(bank, ll, rh, start=False, stop=last)

        def cols(j, split, free, h_ready=None):
            pe.wait_ge(wl_done, split)
            if free is not None:
                pe.wait_ge(bank_free, free)
            for c in range(DC):
                if h_ready is not None:
                    pe.wait_ge(hl_done, h_ready + c + 1)
                mm = three(psum[:, j, :], (wH[:, j, c, :], wL[:, j, c, :]), (hH[:, c, :], hL[:, c, :]), c == 0, c == DC - 1)
            mm.then_inc(bank_done, 1)

        def rows(g, tokens_first=False):
            order = [(tt, c) for tt in range(TT) for c in range(DC)] if tokens_first else \
                    [(tt, c) for j in range(4) for tt in range(TT) for c in (2 * j, 2 * j + 1)]
            for tt, c in order:
                j, part, tok = c // 2, slice(c % 2 * 4, c % 2 * 4 + 4), slice(tt * P, (tt + 1) * P)
                if tt == 0 and c % 2 == 0:
                    pe.wait_ge(wl_done, 4 * g + j + 1)
                if c == 0:
                    pe.wait_ge(bank_free, 4 * g + tt - 3)
                mm = three(psum[:, tt, :], (hH[:, c, tok], hL[:, c, tok]), (wH[:, j, part, :], wL[:, j, part, :]), c == 0, c == DC - 1)
                if tt == TT - 1 and c % 2:
                    mm.then_inc(bank_done, 1)
                elif c == DC - 1:
                    mm.then_inc(rows_done, 1)

        def side_bank(m):
            if m >= 4:
                pe.wait_ge(*evacuated(m - 4))
            return side(m)

        def norm_transposes(name, ph):
            pe.wait_ge(xn_done, 4 * ph + 4)
            for c in range(DC):
                b = side_bank(side_at(name, c))
                for tt in range(TT):
                    mm = pe.transpose(b[:, tt * P:(tt + 1) * P], xn[:, tt, c * P:(c + 1) * P], ident)
                mm.then_inc(side_done, 1)

        def hh(h):
            return slice(h % 2 * 64, h % 2 * 64 + 64)

        def scores(c):
            b = side_bank(side_at("S", c))
            if c == 0:
                for q in range(4):
                    pe.wait_ge(*evacuated(side_at("QKT", q)))
            for h in range(H):
                mm = pe.matmul(b[:, h * P:(h + 1) * P], kT[:, h // 2, c * P:(c + 1) * P],
                               qz[:, h, c * P:(c + 1) * P], start=True, stop=True)
            mm.then_inc(side_done, 1)

        def chunk(c):
            b = side_bank(side_at("O", c))
            pe.wait_ge(*evacuated(side_at("S", c)))
            if c:
                pe.wait_ge(*evacuated(side_at("ST", c - 1)))
            for h in range(H):
                o = b[:, h * P:(h + 1) * P]
                mm = pe.matmul(o, scm[:, c % 2, h * P:(h + 1) * P], vt[:, c, h * P:(h + 1) * P], start=True, stop=(c == 0))
                if c:
                    mm = pe.matmul(o, qdz[:, h, c * P:(c + 1) * P], stat[:, (c - 1) % 2, h // 2, :],
                                   start=False, stop=True)
            mm.then_inc(side_done, 1)
            if c < TT - 1:
                b = side_bank(side_at("ST", c))
                pe.wait_ge(kd_done, 1)
                for h in range(H):
                    mm = pe.matmul(b[hh(h), h // 2 * P:(h // 2 + 1) * P], kd[:, c, h * 64:(h + 1) * 64],
                                   vt[:, c, h * P:(h + 1) * P], start=True, stop=True)
                mm.then_inc(side_done, 1)

        def tile(n, h_ready=None):
            cols(n % 4, n + 1, n - 3 if n >= 4 else None, h_ready)

        pe.wait_ge(cst_in, 16)
        norm_transposes("XT", 0)
        for n in range(4 * UVAL, 4 * UGATE + 4):
            tile(n, 0 if n == 0 else None)
        rows(QK)
        rows(VV)
        pe.wait_ge(rot_done, TT)
        for b in range(4):
            bank = side_bank(side_at("QKT", b))
            for tt in range(TT):
                mm = pe.transpose(bank[:, tt * P:(tt + 1) * P], qkrot[:, tt, b * P:(b + 1) * P], ident)
            mm.then_inc(side_done, 1)
        for n in range(4 * GRET, 4 * GRET + 4):
            tile(n)
        scores(0)
        pe.wait_ge(qd_done, H)
        for c in range(TT):
            tile(4 * GATE_A + c)
            chunk(c)
            if c < TT - 1:
                scores(c + 1)
        for n in range(4 * GATE_A + 4, 4 * GATE_A + 8):
            tile(n)
        pe.wait_ge(y_done, TT)
        for h in range(H):
            b = side_bank(side_at("YT", h))
            for tt in range(TT):
                mm = pe.transpose(b[:, tt * P:(tt + 1) * P], osb[:, tt, h * P:(h + 1) * P], ident)
            mm.then_inc(side_done, 1)
        for n in range(4 * GATE_B, 4 * GATE_B + 4):
            tile(n)

        def channel_mean(name, src):
            b = side_bank(side_at(name))
            for ch in range(CH):
                mm = pe.matmul(b, ones, src[:, ch, :], start=(ch == 0), stop=(ch == CH - 1))
            mm.then_inc(side_done, 1)

        pe.wait_ge(conv_step, TAPS * CH)
        channel_mean("MU", cacc)
        for n in range(4 * GATE_B + 4, 4 * GATE_B + 8):
            tile(n)
            if n == 4 * GATE_B + 6:
                pe.wait_ge(sqc_done, CH)
                channel_mean("VAR", sqc)
        for i in range(DC):
            n = 4 * PROJ + i
            pe.wait_ge(wl_done, n + 1)
            pe.wait_ge(bank_free, n - 3)
            b = side_bank(side_at("PB", i))
            for c in range(DC):
                if i == 0:
                    pe.wait_ge(yl_done, c + 1)
                mm = three(stream(n) if c < 4 else b, (wH[:, n % 4, c, :], wL[:, n % 4, c, :]), (yH[:, c, :], yL[:, c, :]),
                           c % 4 == 0, c % 4 == 3)
                if c == 3:
                    mm.then_inc(side_done, 1)
            mm.then_inc(bank_done, 1)
        pe.wait_ge(hl_done, 2 * DC)
        rows(WOUT)
        rows(WOUT + 1, tokens_first=True)
        norm_transposes("HT", 1)

        def query_scores(hp):
            b = side_bank(side_at("SC", hp))
            if hp == 0:
                pe.wait_ge(key_in, 16)
            pe.wait_ge(bank_free, 4 * QUERY + hp + 1)
            for tt in range(TT):
                mm = pe.matmul(b[:, tt * P:(tt + 1) * P], qT[:, hp, tt * P:(tt + 1) * P], keyT[:, hp, :], start=True, stop=True)
            mm.then_inc(side_done, 1)

        for hp in range(HP):
            tile(4 * QUERY + hp, 2 * DC if hp == 0 else None)
            if hp:
                query_scores(hp - 1)
        for u in range(4 * AHEAD):
            tile(FRONT + u)
            if u == 0:
                query_scores(HP - 1)

        for tt in range(TT):
            b = side_bank(side_at("ET", tt))
            pe.wait_ge(pick_done, 2 * tt + 3)
            for q, src in enumerate((e1f, e2f, gtf)):
                mm = pe.transpose(b[:, q * P:(q + 1) * P], src[:, tt, :], ident)
            mm.then_inc(side_done, 1)

        with pe.Fori(0, NBLK) as blk:
            for k in range(PER_BLK):
                m = GATE0 + k
                s, v = evacuated(m - 4)
                pe.wait_ge(s, v + blk * (PER_BLK // 4))
                pe.wait_ge(ohg_done, blk * PER_BLK + k + 2)
                for q in range(BATCH):
                    mm = pe.matmul(side(m)[:, q * P:(q + 1) * P], oh[:, k % 4, 0, q, :], oh[:, k % 4, 1, q, :], start=True, stop=True)
                mm.then_inc(side_done, 1)

        def second(i, ops):
            v_hi, v_lo, a_hi, a_lo = ops
            for q in range(2 * TT):
                m = OUT0 + q
                s, v = evacuated(m - 4)
                pe.wait_ge(s, v + i * 2)
                tok, half = slice(q // 2 * P, (q // 2 + 1) * P), slice(q % 2 * 512, q % 2 * 512 + 512)
                for j in range(4):
                    if q == 0:
                        pe.wait_ge(vl_done, i * 4 + j + 1)
                        pe.wait_ge(al_done, i * 4 + j + 1)
                    mm = three(side(m), (a_hi[:, j, tok], a_lo[:, j, tok]), (v_hi[:, j, half], v_lo[:, j, half]), j == 0, j == 3)
                mm.then_inc(side_done, 1)

        with pe.Fori(0, LAST) as i:
            for j in range(4):
                n = FRONT + 4 * AHEAD + j
                cols(j, i * 4 + n + 1, i * 4 + n - 3)
            second(i, operands(None))
        with pe.Fori(0, AHEAD // 2) as i2:
            for k in range(2):
                second(i2 * 2 + LAST + k, operands(LAST + k))

    @block.scalar
    def _(act):
        def norm_stats(ph):
            for tt in range(TT):
                if ph == 0:
                    act.wait_ge(x_in[tt], 16)
                else:
                    act.wait_ge(bank_free, 4 * WOUT + 4 + tt + 1)
                if ph or tt:
                    act.wait_ge(sq_done, 4 * ph + tt)
                act.activation(junk[:, :], res[:, tt, :], ACT.Square, accum_out=ssq[:, tt:tt + 1]).then_inc(sq_done, 1)

        def norm_root(ph):
            act.wait_ge(ms_done, 1 + 2 * ph)
            act.activation(rst, rst, ACT.Sqrt).then_inc(rt_done, 1)

        def norm_hi(name, ph):
            for c in range(DC):
                act.wait_ge(*evacuated(side_at(name, c)))
                act.activation(hH[:, c, :], hraw[:, c, :], ACT.Copy).then_inc(hh_done, 1)

        def w_hi(j, landed, freed):
            act.wait_ge(w_in[j], landed)
            if freed is not None:
                act.wait_ge(bank_done, freed)
            act.activation(wH[:, j, :, :], wraw[:, j, :, :], ACT.Copy).then_inc(wh_done, 1)

        def w_hi_tile(n):
            w_hi(n % 4, 16 * (n // 4 + 1), n - 3 if n >= 4 else None)

        def copy_out(n, dst, func=ACT.Copy):
            act.wait_ge(*bank_ready(n))
            act.activation(dst, stream(n), func).then_inc(bank_free, 1)

        def side_out(m, dst):
            act.wait_ge(side_done, m + 1)
            act.activation(dst, side(m), ACT.Copy).then_inc(side_free[m % 4], 1)

        def score_out(hp):
            if hp >= 8:
                act.wait_ge(topk_head, hp // 2 - 3)
            side_out(side_at("SC", hp), sc[:, hp // 2 % 4, hp % 2, :, :].rearrange("p t n -> p (t n)"))

        norm_stats(0)
        w_hi_tile(0)
        norm_root(0)
        w_hi_tile(1)
        norm_hi("XT", 0)
        nxt = 2
        for n in range(FRONT + 4 * AHEAD):
            g, j = n // 4, n % 4
            used = 4 * g + 3 if g in ROWS else n
            while nxt < FRONT + 4 * AHEAD + 3 and nxt - 4 < used:
                w_hi_tile(nxt)
                nxt += 1
            if g == UVAL:
                copy_out(n, val[:, j, :])
            elif g == UGATE:
                copy_out(n, sg[:, j, :], ACT.Sigmoid)
            elif g == QK:
                copy_out(n, qkraw[:, j, :])
            elif g == VV:
                copy_out(n, vt[:, j, :])
            elif g == GRET:
                copy_out(n, gs[:, j, :], ACT.Silu)
            elif g in (GATE_A, GATE_A + 1):
                copy_out(n, sa[:, n - 4 * GATE_A, :], ACT.Sigmoid)
            elif g in (GATE_B, GATE_B + 1):
                copy_out(n, sb[:, n - 4 * GATE_B, :], ACT.Sigmoid)
            elif g in (PROJ, PROJ + 1):
                i = n - 4 * PROJ
                act.wait_ge(mix_done, i + 1)
                act.activation(hH[:, i, :], sa[:, i, :], ACT.Copy).then_inc(hh_done, 1)
            elif QUERY <= g < EXPERTS:
                hp = n - 4 * QUERY
                copy_out(n, qT[:, hp, :])
                if hp:
                    score_out(hp - 1)
            elif g >= EXPERTS:
                u = n - FRONT
                copy_out(n, gel[:, (u // 4 + 1) % 4, j, :], ACT.Gelu)
                if u == 0:
                    score_out(HP - 1)
                if u == 6:
                    act.wait_ge(exp_in, 1)
                    act.activation(best[:, :, :, :].rearrange("p a b c -> p (a b c)"), dec[:, 3, :], ACT.Exp).then_inc(exp_done, 1)
            if n == 4 * VV + 3:
                for b in range(2):
                    m = side_at("QKT", b)
                    act.wait_ge(side_done, m + 1)
                    act.activation(qz[:, 2 * b, :], side(m), ACT.Copy, scale=C("half")[:, 0:1])
                    act.activation(qz[:, 2 * b + 1, :], side(m), ACT.Copy, scale=C("half")[:, 1:2]).then_inc(side_free[m % 4], 1)
                for b in range(2):
                    side_out(side_at("QKT", 2 + b), kT[:, b, :])
            if g == GATE_A:
                side_out(side_at("O", j), osb[:, j, :])
            if n == 4 * GATE_A + 5:
                act.wait_ge(ms_done, 2)
                act.activation(grs, grs, ACT.Sqrt).then_inc(rt_done, 1)
            if n == 4 * GATE_B:
                for h in range(H):
                    act.wait_ge(*evacuated(side_at("YT", h)))
                    act.activation(yH[:, h, :], gs[:, h, :], ACT.Copy).then_inc(yh_done, 1)
            if n == 4 * GATE_B + 4:
                for ch in range(CH):
                    act.wait_ge(cen_done, ch + 1)
                    act.activation(sqc[:, ch, :], cacc[:, ch, :], ACT.Square).then_inc(sqc_done, 1)
            if n == 4 * GATE_B + 6:
                act.wait_ge(*evacuated(side_at("VAR")))
                act.activation(rsd[:, :], rsd[:, :], ACT.Sqrt).then_inc(rt_done, 1)
            if n == 4 * GATE_B + 7:
                for ch in range(CH):
                    act.wait_ge(cn_done, ch + 1)
                    act.activation(sqc[:, ch, :], cacc[:, ch, :], ACT.Silu, bias=PR("ln_b", ch), scale=PR("ln_g", ch)).then_inc(yc_done, 1)
                for ch in range(CH):
                    act.wait_ge(yc_done, ch + 1)
                    act.activation(yH[:, 4 + ch, :], sqc[:, ch, :], ACT.Copy).then_inc(yh_done, 1)
            if n == 4 * WOUT + 7:
                norm_stats(1)
                norm_root(1)
                norm_hi("HT", 1)

        for tt in range(TT):
            m = side_at("ET", tt)
            act.wait_ge(side_done, m + 1)
            act.activation(eT[:, :, tt * P:(tt + 1) * P], side(m)[:, 0:3 * P].rearrange("p (q t) -> p q t", q=3),
                           ACT.Copy).then_inc(side_free[m % 4], 1)

        act.activation(iota_psum, iota, ACT.Copy).then_inc(iota_done, 1)

        def stage_block(s, b2, first):
            if not first:
                act.wait_ge(stored[s], b2 * 16)
            for k in range(PER_BLK):
                m = GATE0 + s * PER_BLK + k
                act.wait_ge(side_done, b2 * (2 * PER_BLK) + m + 1)
                act.activation(stage[:, s, :, k * BATCH:(k + 1) * BATCH].rearrange("p e t -> p t e"),
                               side(m).rearrange("p (t e) -> p t e", t=BATCH), ACT.Copy).then_inc(side_free[m % 4], 1)

        for s in range(2):
            stage_block(s, 0, True)
        with act.Fori(1, NBLK // 2) as b2:
            for s in range(2):
                stage_block(s, b2, False)

        def group(i, k, ops, free, first_prod=True, w_ahead=4):
            for j in range(4):
                n = FRONT + 4 * AHEAD + j
                if j < w_ahead:
                    w_hi((n + 3) % 4, i * 16 + 16 * ((n + 3) // 4 + 1), i * 4 + n)
                act.wait_ge(v_in[j], i * 16 + 16)
                act.wait_ge(*free)
                act.activation(ops[0][:, j, :], vraw[:, j, :], ACT.Copy).then_inc(vh_done, 1)
                act.wait_ge(a_done, i * 4 + j + 1)
                act.activation(ops[2][:, j, :], gel[:, (k + 1) % 4, j, :], ACT.Copy).then_inc(ah_done, 1)
                if first_prod:
                    act.wait_ge(bank_done, i * 4 + n + 1)
                    act.wait_ge(al_done, i * 4 + j + 1)
                    act.activation(gel[:, (k + AHEAD + 1) % 4, j, :], psum[:, j, :], ACT.Gelu).then_inc(bank_free, 1)

        for i in range(4):
            group(i, i, operands(None), (side_done, OUT0 + 8 * i))
        with act.Fori(1, LAST // 4 - 1) as i4:
            for k in range(4):
                group(i4 * 4 + k, k, operands(None), (side_done, i4 * 32 + OUT0 + 8 * k))
        for i in range(LAST - 4, LAST):
            group(i, i % 4, operands(None), (side_done, OUT0 + 8 * i), w_ahead=min(4, N_U - 4 * (i + AHEAD) - 3))
        for i in range(LAST, GROUPS):
            free = (bank_done, FRONT + N_U) if i == LAST else (side_done, OUT0 + 8 * (i - 1))
            group(i, i % 4, operands(i), free, first_prod=False, w_ahead=0)

        for tt in range(TT):
            for half in range(2):
                act.wait_ge(*evacuated(OUT0 + 8 * (GROUPS - 1) + 2 * tt + half))
            act.wait_ge(sq_done, 8 + tt)
            act.activation(fjunk[:, :], res[:, tt, :], ACT.Square, accum_out=ssq[:, tt:tt + 1]).then_inc(sq_done, 1)
            act.wait_ge(ms_done, 4 + tt)
            act.activation(rst[:, tt:tt + 1], rst[:, tt:tt + 1], ACT.Sqrt).then_inc(rt_done, 1)


    @block.gpsimd
    def _(pool):
        steps = [0]

        def step(ins):
            ins.then_inc(pool_step, 1)
            steps[0] += 1
            return steps[0]

        def w_lo(j, count):
            pool.wait_ge(wh_done, count)
            pool.tensor_tensor(wL[:, j, :, :], wraw[:, j, :, :], f(wH[:, j, :, :]), ALU.subtract).then_inc(wl_done, 1)

        def rotate(tt):
            pool.wait_ge(bank_free, 4 * QK + tt + 1)
            v = qkraw[:, tt, :].rearrange("p (s h f i) -> p s h f i", s=2, h=H, f=2)
            o = qkrot[:, tt, :].rearrange("p (s h f i) -> p s h f i", s=2, h=H, f=2)
            r = [rtmp[:, q, :].rearrange("p (s h i) -> p s h i", s=2, h=H) for q in range(4)]
            cs, sn = (bc(tab[:, tt, :, :], 2, H) for tab in (cosv, sinv))
            if tt:
                pool.wait_ge(pool_step, 5 * tt)
                pool.wait_ge(rot_done, tt)
            step(pool.tensor_tensor(r[0], v[:, :, :, 0, :], cs, ALU.mult))
            n1 = step(pool.tensor_tensor(r[1], v[:, :, :, 1, :], sn, ALU.mult))
            step(pool.tensor_tensor(r[2], v[:, :, :, 0, :], sn, ALU.mult))
            n2 = step(pool.tensor_tensor(r[3], v[:, :, :, 1, :], cs, ALU.mult))
            pool.wait_ge(pool_step, n1)
            pool.wait_ge(pool_step, n2)
            step(pool.tensor_tensor(o[:, :, :, 0, :], r[0], r[1], ALU.subtract))
            pool.tensor_tensor(o[:, :, :, 1, :], r[2], r[3], ALU.add).then_inc(rot_done, 1)

        pool.memset(cpad[:, :, 0:TAPS - 1], 0.0).then_inc(pad_done, 1)
        for n in range(FRONT + 4 * AHEAD + 3):
            w_lo(n % 4, n + 1)
            if n == 4 * VV + 3:
                pool.wait_ge(cst_in, 16)
                for tt in range(TT):
                    rotate(tt)
            if n == 4 * GRET + 3:
                pool.wait_ge(rot_done, TT)
                pool.tensor_tensor(kd[:, :, :].rearrange("p t (h d) -> p t h d", h=H),
                                   qkrot[:, :, 256:512].rearrange("p t (h d) -> p t h d", h=H),
                                   bc(bc(C("kdec"), 1, TT), 3, 64), ALU.mult).then_inc(kd_done, 1)
        for q in range(2 * TT):
            tt, w = q // 2, q % 2
            pool.wait_ge(hot_done, q + 1)
            pool.tensor_tensor(hot[:, w, :, :, :], hot[:, w, :, :, :], bc((i1f, i2f)[w][:, tt, :, :], 2, TOPK),
                               ALU.mult).then_inc(hotx_done, 1)
        for tt in range(TT):
            pool.wait_ge(*evacuated(side_at("ET", tt)))
        pool.sem_inc(ohg_done, 1)
        with pool.Fori(0, NBLK) as blk:
            wait_now(pool, "pool", ohg_done, blk * PER_BLK + 1)
            pool.tensor_copy(gblk[:, :], eT[:, 2, bass.ds(blk * TBLK, TBLK)]).then_inc(gblk_done, 1)
            wait_now(pool, "pool", gblk_done, blk + 1)
            for k in range(PER_BLK):
                pool.wait_ge(oh_done, blk * PER_BLK + k + 1)
                pool.tensor_tensor(oh[:, k % 4, 1, :, :], oh[:, k % 4, 1, :, :], bc(gblk[:, k * BATCH:(k + 1) * BATCH], 2, P),
                                   ALU.mult).then_inc(ohg_done, 1)
        with pool.Fori(0, (N_U - 4 * AHEAD - 4) // 4) as i:
            for j in range(4):
                n = FRONT + 4 * AHEAD + 3 + j
                w_lo(n % 4, i * 4 + n + 1)
        w_lo((FRONT + N_U - 1) % 4, FRONT + N_U)

    @block.vector
    def _(dve):
        steps = [0]

        def step(ins):
            ins.then_inc(dve_step, 1)
            steps[0] += 1
            return steps[0]

        def norm_scale(ph):
            dve.wait_ge(sq_done, 4 * ph + 4)
            dve.tensor_scalar(rst, ssq, 1.0 / D, RMS_EPS, ALU.mult, ALU.add).then_inc(ms_done, 1)
            dve.wait_ge(rt_done, 1 + 3 * ph)
            dve.wait_ge(dve_step, step(dve.reciprocal(rst, rst)))
            for tt in range(TT):
                dve.tensor_scalar(xn[:, tt, :], res[:, tt, :], rst[:, tt:tt + 1], None, ALU.mult).then_inc(xn_done, 1)

        def norm_raw(name, gain, lo0):
            def lo(c):
                dve.wait_ge(hh_done, lo0 + c + 1)
                dve.tensor_tensor(hL[:, c, :], hraw[:, c, :], f(hH[:, c, :]), ALU.subtract).then_inc(hl_done, 1)
            for c in range(DC):
                m = side_at(name, c)
                dve.wait_ge(side_done, m + 1)
                dve.tensor_scalar(hraw[:, c, :], side(m), PR(gain, c), None, ALU.mult).then_inc(side_free[m % 4], 1)
                if c:
                    lo(c - 1)
            lo(DC - 1)

        def tap(k):
            for ch in range(CH):
                dve.wait_ge(conv_step, k * CH + ch - CH + 1)
                dve.scalar_tensor_tensor(cacc[:, ch, :], cpad[:, ch, bass.ds(k, T)],
                                         prm[:, bass.ds(k + PARAM_AT["dww"][0] + ch * TAPS, 1)],
                                         cacc[:, ch, :], ALU.mult, ALU.add).then_inc(conv_step, 1)

        def mask(c):
            m = side_at("S", c)
            dve.wait_ge(side_done, m + 1)
            dve.tensor_tensor(scm[:, c % 2, :], side(m), C("mask"), ALU.mult).then_inc(side_free[m % 4], 1)

        def next_state(c):
            m = side_at("ST", c)
            dve.wait_ge(side_done, m + 1)
            for b in range(2):
                src, dst = side(m)[:, b * P:(b + 1) * P], stat[:, c % 2, b, :]
                if c == 0:
                    ins = dve.tensor_copy(dst, src)
                else:
                    if b == 0:
                        dve.wait_ge(state_done, c)
                    else:
                        dve.wait_ge(*evacuated(side_at("ST", c - 1)))
                    ins = dve.scalar_tensor_tensor(dst, stat[:, (c - 1) % 2, b, :], C("cdec")[:, b:b + 1], src, ALU.mult, ALU.add)
                ins.then_inc(state_done if b == 0 else side_free[m % 4], 1)

        dve.wait_ge(prm_in, 16)
        norm_scale(0)
        norm_raw("XT", "g_mix", 0)
        dve.wait_ge(pad_done, 1)
        for ch in range(CH):
            dve.wait_ge(bank_free, 4 * UGATE + ch + 1)
            dve.tensor_tensor(cpad[:, ch, TAPS - 1:], val[:, ch, :], sg[:, ch, :], ALU.mult).then_inc(conv_in, 1)
        for ch in range(CH):
            dve.wait_ge(conv_in, ch + 1)
            dve.tensor_scalar(cacc[:, ch, :], cpad[:, ch, 0:T], PR("dww", ch * TAPS), PR("dwb", ch), ALU.mult, ALU.add).then_inc(conv_step, 1)
        with dve.Fori(1, 20) as k:
            tap(k)
        for b in range(2):
            dve.wait_ge(*evacuated(side_at("QKT", b)))
            for h in (2 * b, 2 * b + 1):
                dve.tensor_tensor(qdz[:, h, :].rearrange("p (t n) -> p t n", t=TT), qz[:, h, :].rearrange("p (t n) -> p t n", t=TT),
                                  bc(C("qdec")[:, b * P:(b + 1) * P], 1, TT), ALU.mult).then_inc(qd_done, 1)
        mask(0)
        for c in range(TT - 1):
            next_state(c)
            mask(c + 1)
        with dve.Fori(20, TAPS) as k:
            tap(k)
        for c in range(TT):
            dve.wait_ge(*evacuated(side_at("O", c)))
            for h in range(H):
                n0 = step(dve.bn_stats(bst[:, c * H + h, :], osb[:, c, h * P:(h + 1) * P]))
        for n in range(TT * H):
            dve.wait_ge(dve_step, n0 - TT * H + n + 1)
            last = step(dve.bn_aggr(mv[:, n, :], bst[:, n, :]))
        dve.wait_ge(dve_step, last)
        dve.tensor_scalar(grs, mv[:, :, 1], LN_EPS, None, ALU.add).then_inc(ms_done, 1)
        dve.wait_ge(rt_done, 2)
        dve.wait_ge(dve_step, step(dve.reciprocal(grs, grs)))
        for c in range(TT):
            for h in range(H):
                o = osb[:, c, h * P:(h + 1) * P]
                ins = dve.tensor_scalar(o, o, mv[:, c * H + h, 0:1], grs[:, c * H + h:c * H + h + 1], ALU.subtract, ALU.mult)
            ins.then_inc(y_done, 1)

        def y_lo(c, src):
            dve.wait_ge(yh_done, c + 1)
            dve.tensor_tensor(yL[:, c, :], src, f(yH[:, c, :]), ALU.subtract).then_inc(yl_done, 1)

        for h in range(H):
            m = side_at("YT", h)
            dve.wait_ge(side_done, m + 1)
            dve.scalar_tensor_tensor(gs[:, h, :], side(m), PR("gn", h), gs[:, h, :], ALU.mult, ALU.mult).then_inc(side_free[m % 4], 1)
        for h in range(H):
            y_lo(h, gs[:, h, :])
        m = side_at("MU")
        dve.wait_ge(side_done, m + 1)
        dve.tensor_copy(rsd[:, :], side(m)).then_inc(side_free[m % 4], 1)
        dve.wait_ge(*evacuated(m))
        for ch in range(CH):
            dve.tensor_tensor(cacc[:, ch, :], cacc[:, ch, :], rsd[:, :], ALU.subtract).then_inc(cen_done, 1)
        m = side_at("VAR")
        dve.wait_ge(side_done, m + 1)
        dve.tensor_scalar(rsd[:, :], side(m), LN_EPS, None, ALU.add).then_inc(side_free[m % 4], 1)
        dve.wait_ge(rt_done, 3)
        dve.wait_ge(dve_step, step(dve.reciprocal(rsd[:, :], rsd[:, :])))
        for ch in range(CH):
            dve.tensor_tensor(cacc[:, ch, :], cacc[:, ch, :], rsd[:, :], ALU.mult).then_inc(cn_done, 1)
        for ch in range(CH):
            y_lo(4 + ch, sqc[:, ch, :])

        def mix_lo(i):
            dve.wait_ge(hh_done, DC + i + 1)
            dve.tensor_tensor(hL[:, i, :], sa[:, i, :], f(hH[:, i, :]), ALU.subtract).then_inc(hl_done, 1)

        for i in range(DC):
            m, n = side_at("PB", i), 4 * PROJ + i
            dve.wait_ge(bank_done, n + 1)
            dve.scalar_tensor_tensor(tb[:, i % 2, :], side(m), PR("bproj", i), sb[:, i, :], ALU.add, ALU.mult).then_inc(side_free[m % 4], 1)
            dve.tensor_tensor(sa[:, i, :], stream(n), sa[:, i, :], ALU.mult).then_inc(bank_free, 1)
            dve.wait_ge(*evacuated(m))
            dve.wait_ge(bank_free, n + 1)
            dve.tensor_tensor(sa[:, i, :], sa[:, i, :], tb[:, i % 2, :], ALU.add).then_inc(mix_done, 1)
            if i:
                mix_lo(i - 1)
        mix_lo(DC - 1)
        for g in range(2):
            for tt in range(TT):
                n = 4 * (WOUT + g) + tt
                dve.wait_ge(*bank_ready(n))
                r = res[:, tt, g * 512:(g + 1) * 512]
                dve.tensor_tensor(r, r, stream(n), ALU.add).then_inc(bank_free, 1)
        norm_scale(1)
        norm_raw("HT", "g_ffn", 2 * DC)

        N_STEPS = 68

        def top16(head, slot, t0, q):
            par = slot % 2
            units = [(p, tt) for p in range(2) for tt in range(TT)]
            for p in range(2):
                m = side_at("SC", 2 * slot + p)
                wait_now(dve, "dve", side_free[m % 4], q * 2 + m // 4 + 1)
                for tt in range(TT):
                    dve.max(s16[:, par, p, tt, 0:8], sc[:, slot, p, tt, :]).then_inc(topk, 1)

            if slot == 0:
                wait_now(dve, "dve", side_done, q * 8 + side_at("SC", 3) + 1)

            def ready(u, n):
                if u % 4 == 0:
                    wait_now(dve, "dve", topk, n)

            for u, (p, tt) in enumerate(units):
                ready(u, t0 + u + 4)
                dve.max_index(ix[:, par, p, tt, 0:8], s16[:, par, p, tt, 0:8], sc[:, slot, p, tt, :]).then_inc(topk, 1)
            for u, (p, tt) in enumerate(units):
                ready(u, t0 + 8 + u + 4)
                dve.match_replace(sc[:, slot, p, tt, :], s16[:, par, p, tt, 0:8], sc[:, slot, p, tt, :], NEG).then_inc(topk, 1)
            for u, (p, tt) in enumerate(units):
                ready(u, t0 + 16 + u + 4)
                dve.max(s16[:, par, p, tt, 8:16], sc[:, slot, p, tt, :]).then_inc(topk, 1)
            for u, (p, tt) in enumerate(units):
                ready(u, t0 + 24 + u + 4)
                dve.max_index(ix[:, par, p, tt, 8:16], s16[:, par, p, tt, 8:16], sc[:, slot, p, tt, :])\
                   .then_inc(topk if u < 7 else topk_head, 1)
            for i0, (r0, r1, w) in enumerate(RECTS):
                at0 = sum((b - a) * c for a, b, c in RECTS[:i0])
                o = cand[:, par, :, at0:at0 + (r1 - r0) * w].rearrange("p t (i j) -> p t i j", j=w)
                dve.tensor_tensor(o, bc(s16[:, par, 0, :, r0:r1], 3, w), bc(s16[:, par, 1, :, 0:w], 2, r1 - r0), ALU.add).then_inc(topk, 1)
            wait_now(dve, "dve", topk, t0 + 36)
            dve.tensor_copy(i1f[:, :, bass.ds(head, 1), :].rearrange("p t a k -> p t (a k)"), ix[:, par, 0, :, :]).then_inc(topk, 1)
            wait_now(dve, "dve", topk_head, head + 1)
            dve.tensor_copy(i2f[:, :, bass.ds(head, 1), :].rearrange("p t a k -> p t (a k)"), ix[:, par, 1, :, :]).then_inc(topk, 1)
            t1 = t0 + 46

            def picks(buf, tt, a):
                return buf[:, par, tt, a:a + 8]

            ready(0, t1)
            for tt in range(TT):
                dve.max(picks(b16, tt, 0), cand[:, par, tt, :]).then_inc(topk, 1)
            for tt in range(TT):
                ready(tt, t1 + 4)
                dve.max_index(picks(p16, tt, 0), picks(b16, tt, 0), cand[:, par, tt, :]).then_inc(topk, 1)
            for tt in range(TT):
                ready(tt, t1 + 8)
                dve.match_replace(cand[:, par, tt, :], picks(b16, tt, 0), cand[:, par, tt, :], NEG).then_inc(topk, 1)
            for tt in range(TT):
                ready(tt, t1 + 12)
                dve.max(picks(b16, tt, 8), cand[:, par, tt, :]).then_inc(topk, 1)
            for tt in range(TT):
                ready(tt, t1 + 16)
                dve.max_index(picks(p16, tt, 8), picks(b16, tt, 8), cand[:, par, tt, :]).then_inc(topk, 1)
            for n, (dst, src) in enumerate(((best, b16), (pos, p16))):
                wait_now(dve, "dve", topk, t1 + 16 + 4 * n)
                dve.tensor_copy(dst[:, :, bass.ds(head, 1), :].rearrange("p t a k -> p t (a k)"), src[:, par, :, :]).then_inc(topk, 1)

        with dve.Fori(0, 2) as q:
            for slot in range(4):
                top16(q * 4 + slot, slot, (q * 4 + slot) * N_STEPS, q)

        dve.wait_ge(topk, HEADS * N_STEPS)
        flat = "p a b c -> p (a b c)"
        dve.tensor_tensor(dec[:, 3, :].rearrange("p (a b) -> p a b", b=TOPK), best[:, :, :, :].rearrange("p a b c -> p (a b) c"),
                          best[:, :, :, 0:1].rearrange("p a b c -> p (a b) c").to_broadcast([P, TT * HEADS, TOPK]),
                          ALU.subtract).then_inc(exp_in, 1)
        n_p = step(dve.tensor_copy(dec[:, 0, :], pos[:, :, :, :].rearrange(flat)))
        dve.wait_ge(dve_step, n_p)
        n_i = step(dve.tensor_scalar(irank[:, :], dec[:, 0, :], -46.0, 0.0, ALU.add, ALU.max))
        dve.wait_ge(dve_step, n_i)
        n_j = step(dve.tensor_tensor(jrank[:, :], dec[:, 0, :], irank[:, :], ALU.subtract))
        for q, (b, w) in enumerate([(16, 16), (24, 8), (29, 5), (34, 5), (37, 3), (40, 3), (43, 3), (46, 3)]):
            n_t = step(dve.tensor_scalar(dec[:, 1 + q % 2, :], dec[:, 0, :], float(b), float(-w), ALU.is_ge, ALU.mult))
            dve.wait_ge(dve_step, n_i)
            n_i = step(dve.scalar_tensor_tensor(irank[:, :], dec[:, 0, :], float(b), irank[:, :], ALU.is_ge, ALU.add))
            dve.wait_ge(dve_step, n_j)
            dve.wait_ge(dve_step, n_t)
            n_j = step(dve.tensor_tensor(jrank[:, :], jrank[:, :], dec[:, 1 + q % 2, :], ALU.add))
        dve.wait_ge(dve_step, n_j)

        def compare(q):
            tt, w = q // 2, q % 2
            rank = (irank, jrank)[w][:, tt * P:(tt + 1) * P]
            dve.tensor_tensor(hot[:, w, :, :, :].rearrange("p h k r -> p (h k) r"), bc(rank, 2, TOPK), bc(iota[:, 0:TOPK], 1, P),
                              ALU.is_equal).then_inc(hot_done, 1)

        compare(0)
        compare(1)
        dve.wait_ge(exp_done, 1)
        dve.wait_ge(dve_step, step(dve.tensor_reduce(zs, best[:, :, :, :].rearrange("p a b c -> p (a b) c"), AX.X, ALU.add)))
        dve.wait_ge(dve_step, step(dve.reciprocal(zs, zs)))
        dve.tensor_tensor(gtf[:, :, :].rearrange("p a (b c) -> p (a b) c", c=TOPK), best[:, :, :, :].rearrange("p a b c -> p (a b) c"),
                          bc(zs, 2, TOPK), ALU.mult).then_inc(pick_done, 1)
        for q in range(2 * TT):
            tt, w = q // 2, q % 2
            dve.wait_ge(hotx_done, q + 1)
            dve.tensor_reduce((e1f, e2f)[w][:, tt, :], hot[:, w, :, :, :].rearrange("p h k r -> p (h k) r"), AX.X, ALU.add).then_inc(pick_done, 1)
            if q + 2 < 2 * TT:
                dve.wait_ge(pick_done, q + 2)
                compare(q + 2)

        for tt in range(TT):
            dve.wait_ge(*evacuated(side_at("ET", tt)))
        dve.wait_ge(iota_done, 1)
        with dve.Fori(0, NBLK) as blk:
            for k in range(PER_BLK):
                dve.wait_ge(side_done, blk * PER_BLK + GATE0 + k - 3)
                dve.tensor_tensor(oh[:, k % 4, :, :, :], bc(bc(iota_psum, 1, BATCH), 1, 2),
                                  bc(eT[:, 0:2, bass.ds(blk * TBLK + k * BATCH, BATCH)], 3, P), ALU.is_equal).then_inc(oh_done, 1)

        def group(i, k, ops):
            for j in range(4):
                dve.wait_ge(vh_done, i * 4 + j + 1)
                dve.tensor_tensor(ops[1][:, j, :], vraw[:, j, :], f(ops[0][:, j, :]), ALU.subtract).then_inc(vl_done, 1)
                if j == 0:
                    dve.wait_ge(d_in, i * 16 + 16)
                g = gel[:, (k + 1) % 4, j, :]
                dve.wait_ge(bank_free, i * 4 + FRONT + j + 1)
                dve.tensor_tensor(g.rearrange("p (b t) -> p b t", t=TBLK), g.rearrange("p (b t) -> p b t", t=TBLK), dg[:, :, j, :],
                                  ALU.mult).then_inc(a_done, 1)
                dve.wait_ge(ah_done, i * 4 + j + 1)
                dve.tensor_tensor(ops[3][:, j, :], g, f(ops[2][:, j, :]), ALU.subtract).then_inc(al_done, 1)
            for q in range(2 * TT):
                m = OUT0 + q
                dve.wait_ge(side_done, i * 8 + m + 1)
                r = res[:, q // 2, q % 2 * 512:q % 2 * 512 + 512]
                dve.tensor_tensor(r, r, side(m), ALU.add).then_inc(side_free[m % 4], 1)

        with dve.Fori(0, LAST // 4) as i4:
            for k in range(4):
                group(i4 * 4 + k, k, operands(None))
        for i in range(LAST, GROUPS):
            group(i, i % 4, operands(i))
        dve.wait_ge(gfin_in, 16)
        for tt in range(TT):
            one = rst[:, tt:tt + 1]
            dve.wait_ge(sq_done, 8 + tt + 1)
            dve.tensor_scalar(one, ssq[:, tt:tt + 1], 1.0 / D, RMS_EPS, ALU.mult, ALU.add).then_inc(ms_done, 1)
            dve.wait_ge(rt_done, 5 + tt)
            dve.wait_ge(dve_step, step(dve.reciprocal(one, one)))
            dve.scalar_tensor_tensor(res[:, tt, :], res[:, tt, :], one, gfb[:, :], ALU.mult, ALU.mult).then_inc(fin_done, 1)

    ctx.close()


def constants():
    import numpy as np
    gamma = 1.0 - 2.0 ** (-5.0 - np.arange(H, dtype=np.float64))
    inv = (1.0 / (np.float32(10000.0) ** (np.arange(32, dtype=np.float32) / np.float32(32)))).astype(np.float32)
    ang = (np.arange(T, dtype=np.float32)[:, None] * inv[None, :]).astype(np.float64)
    scale = np.array([1.0, 64 ** -0.5])
    rope = lambda a: (a[:, None, :] * scale[None, :, None]).reshape(TT, P, 64).transpose(1, 0, 2).reshape(P, -1)
    n = np.arange(P, dtype=np.float64)
    diff = n[None, :] - n[:, None]
    mask = np.stack([np.where(diff >= 0, g ** np.maximum(diff, 0), 0.0) for g in gamma], 1)
    pair = np.repeat(gamma.reshape(2, 2).T, 64, axis=0)
    parts = {
        "ident": np.eye(P), "iota": np.tile(n, (P, 1)), "ones": np.full((P, P), 1.0 / 512),
        "cos": rope(np.cos(ang)), "sin": rope(np.sin(ang)), "mask": mask.reshape(P, -1),
        "qdec": (pair[:, :, None] ** (n + 1.0)).reshape(P, -1),
        "kdec": gamma[None, :] ** (P - 1.0 - n[:, None]), "cdec": pair ** P, "half": np.stack([n < 64, n >= 64], 1),
    }
    return np.concatenate([parts[name] for name, _ in CONSTS], axis=1).astype(np.float32)


def kernel(**inputs):
    import numpy as np
    import concourse.bacc as bacc
    from concourse.bass_utils import run_bass_kernel_spmd as run

    a = {k: np.asarray(v) for k, v in inputs.items()}

    def tiles(w):
        k, n = w.shape
        return w.reshape(k // P, P, n // P, P).transpose(2, 1, 0, 3).reshape(n // P, P, -1)

    def cols(v):
        return v.reshape(-1, P).T

    def row_tiles(w):
        return w.reshape(4, 2, P, -1, 512).transpose(3, 0, 2, 1, 4).reshape(-1, P, D)

    w_in = a["w_in"][0]
    qk, v, g_ret, u_val, u_gate, gates = np.split(w_in, [512, 1024, 1536, 2048, 2560], axis=1)
    proj = tiles(np.concatenate([a["w_ret_proj"][0], a["w_conv_proj"][0]], axis=0))
    params = [cols(a["rms_mix_g"][0]), cols(a["rms_ffn_g"][0]), cols(a["ret_gn_g"][0].reshape(-1)), cols(a["conv_ln_g"][0]),
              cols(a["conv_ln_b"][0]), cols(a["conv_dw_b"][0]), cols(a["b_conv_proj"][0]),
              a["conv_dw_w"][0].reshape(TAPS, CH, P).transpose(2, 1, 0).reshape(P, -1)]
    arrays = {
        "x": a["x"][0],
        "wfront": np.concatenate([tiles(u_val), tiles(u_gate), row_tiles(qk), row_tiles(v), tiles(g_ret), tiles(gates), proj,
                                  row_tiles(a["w_out"][0]), tiles(a["w_query"][0])], axis=0),
        "ut": a["peer_u"][0].reshape(P, NKEY, DC, P).transpose(1, 3, 2, 0).reshape(NKEY, P, D),
        "peer_v": a["peer_v"][0].reshape(P, NKEY, D),
        "keys": a["peer_sub_keys"][0].transpose(3, 0, 1, 2).reshape(P, -1),
        "consts": constants(),
        "params": np.concatenate(params, axis=1),
        "gfin": np.broadcast_to(a["rms_final_g"], (P, D)),
    }
    arrays = {k: np.ascontiguousarray(v) for k, v in arrays.items()}
    nc = bacc.Bacc("TRN2", target_bir_lowering=False, num_devices=1)
    args = [nc.dram_tensor(k, v.shape, F32, kind="ExternalInput").ap() for k, v in arrays.items()]
    out = nc.dram_tensor("out", (T, D), F32, kind="ExternalOutput").ap()
    build(nc, *args, out)
    r = run(nc, [arrays], core_ids=[0])
    return r.results[0]["out"].reshape(1, T, D)
```

```python
from contextlib import ExitStack

import concourse.bass as bass
from concourse import mybir

P = 128
T = 512
TT = T // P
D = 1024
DC = D // P
H = 4
CH = 4
TAPS = 31
HP = 16
HEADS = 8
TOPK = 16
NKEY = 128

F32 = mybir.dt.float32
F32R = mybir.dt.float32r
BF16 = mybir.dt.bfloat16
U32 = mybir.dt.uint32
ALU = mybir.AluOpType
ACT = mybir.ActivationFunctionType
AX = mybir.AxisListType
NEG = -3.0e38
RMS_EPS, LN_EPS = 1e-6, 1e-5

UVAL, UGATE, QK, VV, GRET = 0, 1, 2, 3, 4
GATE_A, GATE_B, PROJ, WOUT, QUERY, EXPERTS = 5, 7, 9, 11, 13, 17
FRONT = 4 * EXPERTS
N_U = NKEY
GROUPS = N_U // 4
AHEAD = 4
ROWS = (QK, VV, WOUT, WOUT + 1)

SIDE = [("XT", i) for i in range(2 * TT)] + [("QKT", b) for b in range(4)]
for _c in range(TT):
    SIDE += [("S", 0)] if _c == 0 else []
    SIDE += [("O", _c)]
    SIDE += [("ST", _c), ("S", _c + 1)] if _c < TT - 1 else []
SIDE += [("YT", h) for h in range(H)] + [("MU", 0), ("VAR", 0)]
SIDE += [("PB", i) for i in range(DC)] + [("HT", i) for i in range(2 * TT)]
SIDE += [("SC", i) for i in range(HP)] + [("ET", t) for t in range(TT)]
SIDE_AT = {name: m for m, name in enumerate(SIDE)}
GATE0 = len(SIDE)
BATCH = 4
NBATCH = T // BATCH
NB = P // BATCH
TBLK = 32
PER_BLK = TBLK // BATCH
NBLK = T // TBLK
OUT0 = GATE0 + NBATCH
SEGMENTS = 4
SEG2 = NBLK // 2 // SEGMENTS
MID = FRONT + 4 * AHEAD - SEGMENTS
LAST = GROUPS - AHEAD

RECTS = [(0, 1, 16), (1, 2, 8), (2, 4, 5), (4, 8, 3), (8, 16, 1)]
NCAND = sum((b - a) * w for a, b, w in RECTS)

CONSTS = [("ident", 128), ("iota", 128), ("ones", 128), ("cos", TT * 64), ("sin", TT * 64), ("mask", H * 128),
          ("qdec", 256), ("kdec", H), ("cdec", 2), ("half", 2)]
PARAMS = [("g_mix", DC), ("g_ffn", DC), ("gn", H), ("ln_g", CH), ("ln_b", CH), ("dwb", CH), ("bproj", DC),
          ("dww", CH * TAPS)]


def offsets(table):
    at, out = 0, {}
    for name, n in table:
        out[name] = (at, n)
        at += n
    return out, at


N_SMALL = 152
CONST_AT, N_CONST = offsets(CONSTS)
PARAM_AT, N_PARAM = offsets(PARAMS)
N_EARLY = CONST_AT["cos"][0]


def build(nc, x, wfront, ut, peer_v, keys, consts, params, gfin, out):
    spill = nc.dram_tensor("gates_spill", (P, NBLK, NKEY, TBLK), F32, kind="Internal").ap()
    KB = 1024
    base = (nc.sbuf_base + 31) // 32 * 32

    def at(name, shape, kb, dt=F32):
        return nc.alloc_sbuf_tensor_at(name, shape, dt, offset=base + int(kb * KB))

    res = at("res", [P, TT, D], 0)
    hH = at("hH", [P, DC, T], 16, F32R)
    hL = at("hL", [P, DC, T], 32, F32R)
    wraw = at("wraw", [P, 4, DC, P], 48)
    gfb = at("gfb", [P, D], 48)
    wH = at("wH", [P, 4, DC, P], 64, F32R)
    fjunk = at("fjunk", [P, D], 64)
    wL = at("wL", [P, 4, DC, P], 80, F32R)
    cst = at("cst", [P, N_CONST], 96)
    prm_kb = 96 + (N_CONST + 7) // 8 * 32 / KB
    small_kb = prm_kb + (N_PARAM + 7) // 8 * 32 / KB
    prm = at("prm", [P, N_PARAM], prm_kb)
    small = at("small", [P, N_SMALL], small_kb)
    W = 103 + 25 / 32
    assert small_kb + N_SMALL * 4 / KB <= W
    qkraw = at("qkraw", [P, TT, 512], W + 0)
    qkrot = at("qkrot", [P, TT, 512], W + 8)
    sa = at("sa", [P, DC, T], W + 0)
    vt = at("vt", [P, TT, 512], W + 16)
    gs = at("gs", [P, H, T], W + 24)
    yL = at("yL", [P, DC, T], W + 16, F32R)
    kT = at("kT", [P, 2, T], W + 32)
    qz = at("qz", [P, H, T], W + 36)
    kd = at("kd", [P, TT, 256], W + 44)
    sb = at("sb", [P, DC, T], W + 32)
    rtmp = at("rtmp", [P, 4, 256], W + 48)
    scm = at("scm", [P, 2, 512], W + 48)
    stat = at("stat", [P, 2, 2, 128], W + 52)
    rsd = at("rsd", [P, T], W + 50)
    val = at("val", [P, CH, T], W + 54)
    qdz = at("qdz", [P, H, T], W + 54)
    sqc = at("sqc", [P, CH, T], W + 54)
    tb = at("tb", [P, 2, T], W + 54)
    cpad = at("cpad", [P, CH, T + TAPS - 1], W + 62)
    sg = at("sg", [P, CH, T], W + 71)
    cacc = at("cacc", [P, CH, T], W + 71)
    yH = at("yH", [P, DC, T], W + 79, F32R)
    osb = at("osb", [P, TT, 512], W + 95)
    hraw = at("hraw", [P, DC, T], W + 32)
    junk = at("junk", [P, D], W + 48)
    rdiag = at("rdiag", [P, TT, P], W + 52)
    keyT = at("keyT", [P, HP, NKEY], W + 0)
    gtf = at("gtf", [P, TT, P], W + 4)
    s16 = at("s16", [P, 2, 2, TT, TOPK], W + 14)
    ix = at("ix", [P, 2, 2, TT, TOPK], W + 15, U32)
    qT = at("qT", [P, HP, T], W + 16)
    dec = at("dec", [P, 4, TT * P], W + 24)
    stage = at("stage", [P, 2, NKEY, TBLK], W + 16)
    sc = at("sc", [P, 4, 2, TT, NKEY], W + 48)
    prod = at("prod", [P, 2, TOPK, T], W + 32, BF16)
    cand = at("cand", [P, 2, TT, NCAND], W + 64)
    b16 = at("b16", [P, 2, TT, TOPK], W + 65.75)
    p16 = at("p16", [P, 2, TT, TOPK], W + 66.25, U32)
    oh = at("oh", [P, 4, 2, BATCH, P], W + 48)
    eT = at("eT", [P, T // BATCH, 3, BATCH], W + 64)
    identb = at("identb", [P, P], W + 70.25, BF16)
    dist = at("dist", [P, 2, P], W + 70.5)
    i1f = at("i1f", [P, TT, HEADS, TOPK], W + 16)
    i2f = at("i2f", [P, TT, HEADS, TOPK], W + 18)
    best = at("best", [P, TT, HEADS, TOPK], W + 20)
    pos = at("pos", [P, TT, HEADS, TOPK], W + 22)
    irank = at("irank", [P, TT * P], W + 22)
    jrank = at("jrank", [P, TT * P], W + 6)
    vraw = at("vraw", [P, 4, D], W + 0)
    vH = at("vH", [P, 4, D], W + 16, F32R)
    vL = at("vL", [P, 4, D], W + 32, F32R)
    aH = at("aH", [P, 4, T], W + 48, F32R)
    aL = at("aL", [P, 4, T], W + 56, F32R)
    dg = at("dg", [P, NBLK, 4, TBLK], W + 64)
    gel = at("gel", [P, 4, 4, T], W + 72)

    def C(name):
        a, n = CONST_AT[name]
        return cst[:, a:a + n]

    def PR(name, i):
        a, _ = PARAM_AT[name]
        return prm[:, a + i:a + i + 1]

    def bc(ap, axis, n):
        ap = ap.unsqueeze(axis)
        shape = list(ap.shape)
        shape[axis] = n
        return ap.to_broadcast(shape)

    def f(ap):
        return ap.bitcast(F32)

    flat_eT = eT[:, :, :, :].rearrange("p n q b -> p (n q b)")
    ident, iota, ones = C("ident"), C("iota"), C("ones")
    cosv = C("cos").rearrange("p (t s i) -> p t s i", t=TT, s=2)
    sinv = C("sin").rearrange("p (t s i) -> p t s i", t=TT, s=2)
    ssq, rst = small[:, 0:4], small[:, 4:8]
    bst = small[:, 8:104].rearrange("p (n s) -> p n s", s=6)
    mv = small[:, 104:136].rearrange("p (n s) -> p n s", s=2)
    grs = small[:, 136:152]
    zs = small[:, 8:40]

    two_sets = ((vH, vL, aH, aL), (wH[:, :, :, :].rearrange("p j c n -> p j (c n)"), wL[:, :, :, :].rearrange("p j c n -> p j (c n)"),
                                   hH[:, 0:4, :], hL[:, 0:4, :]))

    def operands(i):
        return two_sets[0 if i is None else (i - LAST + 1) % 2]

    ctx = ExitStack()
    psum = ctx.enter_context(nc.psum_tensor("psum", [P, 8, 512], F32))

    iota_psum = psum[:, 3, 0:P]

    def stream(n):
        return psum[:, n % 4, :]

    def side(m):
        return psum[:, 4 + m % 4, :]

    def sem(name):
        return ctx.enter_context(nc.semaphore(name))

    x_in = [sem(f"x_in{i}") for i in range(TT)]
    id_in, cst_in, prm_in, key_in, gfin_in = sem("id_in"), sem("cst_in"), sem("prm_in"), sem("key_in"), sem("gfin_in")
    w_in = [sem(f"w_in{i}") for i in range(4)]
    v_in = [sem(f"v_in{i}") for i in range(4)]
    d_in = sem("d_in")
    wh_done, wl_done = sem("wh_done"), sem("wl_done")
    vh_done, vl_done = sem("vh_done"), sem("vl_done")
    bank_done = sem("bank_done")
    rows_done = sem("rows_done")
    bank_free = sem("bank_free")
    side_done = sem("side_done")
    side_free = [sem(f"side_free{i}") for i in range(4)]
    sq_done, ms_done, rt_done, diag_done = sem("sq_done"), sem("ms_done"), sem("rt_done"), sem("diag_done")
    hh_done, hl_done = sem("hh_done"), sem("hl_done")
    hl2_done = sem("hl2_done")
    pad_done, conv_in, conv_step = sem("pad_done"), sem("conv_in"), sem("conv_step")
    rot_done, kd_done, qd_done, state_done = (sem(n) for n in ("rot_done", "kd_done", "qd_done", "state_done"))
    y_done, yh_done, yl_done = sem("y_done"), sem("yh_done"), sem("yl_done")
    cen_done, sqc_done, cn_done, yc_done = sem("cen_done"), sem("sqc_done"), sem("cn_done"), sem("yc_done")
    mix_done = sem("mix_done")
    topk, topk_head = sem("topk"), sem("topk_head")
    exp_in, exp_done, prod_done, pick_done = (sem(n) for n in ("exp_in", "exp_done", "prod_done", "pick_done"))
    oh_done, ohg_done, iota_done = (sem(n) for n in ("oh_done", "ohg_done", "iota_done"))
    stored = [sem("stored0"), sem("stored1")]
    a_done, ah_done, al_done = sem("a_done"), sem("ah_done"), sem("al_done")
    fin_done, out_done = sem("fin_done"), sem("out_done")
    dve_step, act_step, pool_step = sem("dve_step"), sem("act_step"), sem("pool_step")
    ones_done = sem("ones_done")
    dist_done, ohx_done = sem("dist_done"), sem("ohx_done")

    def bank_ready(n):
        g, j = n // 4, n % 4
        return (rows_done, 3 * ROWS.index(g) + j + 1) if g in ROWS and j < 3 else (bank_done, n + 1)

    def evacuated(m):
        return side_free[m % 4], m // 4 + 1

    def side_at(name, i=0):
        return SIDE_AT[(name, i)]

    passed = {e: sem(f"passed_{e}") for e in ("sp", "act", "dve", "pool")}

    def wait_now(eng, name, s, value):
        eng.wait_ge(s, value)
        eng.sem_inc(passed[name], 1)

    block = ctx.enter_context(nc.Block())

    @block.sync
    def _(sp):
        for tt in range(TT):
            sp.dma_start(res[:, tt, :], x[tt * P:(tt + 1) * P, :]).then_inc(x_in[tt], 16)
            if tt == 0:
                sp.dma_start(cst[:, 0:N_EARLY], consts[:, 0:N_EARLY]).then_inc(id_in, 16)
                sp.dma_start(prm[:, :], params).then_inc(prm_in, 16)

        def load_w(n, src, count):
            if count is not None:
                sp.wait_ge(wh_done, count)
                wait_now(sp, "sp", wl_done, count)
            sp.dma_start(wraw[:, n % 4, :, :].rearrange("p c n -> p (c n)"), src).then_inc(w_in[n % 4], 16)

        for n in range(MID + 7):
            src = wfront[n] if n < FRONT else ut[n - FRONT]
            load_w(n, src, n - 3 if n >= 4 else None)
            if n == 3:
                sp.dma_start(cst[:, N_EARLY:], consts[:, N_EARLY:]).then_inc(cst_in, 16)
            if n == FRONT - 16:
                sp.wait_ge(hl_done, TT + DC)
                sp.dma_start(keyT[:, :, :].rearrange("p a b -> p (a b)"), keys).then_inc(key_in, 16)

        def load_v(j, i):
            sp.dma_start(vraw[:, j, :], peer_v[:, bass.ds(i * 4 + j, 1), :].rearrange("p a d -> p (a d)")).then_inc(v_in[j], 16)

        for tt in range(TT):
            sp.wait_ge(*evacuated(side_at("ET", tt)))
        for j in range(4):
            load_v(j, 0)

        def store(b2):
            for s in range(2):
                for k in range(PER_BLK - 4, PER_BLK):
                    m = GATE0 + s * PER_BLK + k
                    wait_now(sp, "sp", side_free[m % 4], m // 4 + 1 + b2 * (2 * PER_BLK // 4))
                sp.dma_start(spill[:, bass.ds(b2 * 2 + s, 1), :, :].rearrange("p a e t -> p (a e t)"),
                             stage[:, s, :, :].rearrange("p e t -> p (e t)")).then_inc(stored[s], 16)

        with sp.Fori(0, 2) as b2:
            store(b2)
        load_w(MID + 7, ut[MID + 7 - FRONT], MID + 4)
        with sp.Fori(2, NBLK // 2) as b2:
            store(b2)

        def load_d(i):
            sp.dma_start(dg[:, :, :, :].rearrange("p b e t -> p b (e t)"),
                         spill[:, :, bass.ds(i * 4, 4), :].rearrange("p b e t -> p b (e t)")).then_inc(d_in, 16)

        sp.wait_ge(stored[0], 16 * NBLK // 2)
        sp.wait_ge(stored[1], 16 * NBLK // 2)
        load_d(0)
        for n in range(MID + 8, FRONT + 4 * AHEAD + 7):
            load_w(n, ut[n - FRONT], n - 3)
        with sp.Fori(0, GROUPS - AHEAD - 2) as i:
            for j in range(4):
                load_w(j + 3, ut[bass.ds(i * 4 + 4 * AHEAD + j + 7, 1), :, :].rearrange("a p f -> p (a f)"),
                       i * 4 + FRONT + 4 * AHEAD + j + 4)
                sp.wait_ge(vh_done, i * 4 + j + 1)
                wait_now(sp, "sp", vl_done, i * 4 + j + 1)
                load_v(j, i + 1)
            wait_now(sp, "sp", a_done, i * 4 + 4)
            load_d(i + 1)
        for i in range(GROUPS - AHEAD - 2, GROUPS - 1):
            for j in range(4):
                n = 4 * (i + AHEAD) + j + 7
                if n < N_U:
                    load_w(FRONT + n, ut[n], FRONT + n - 3)
                sp.wait_ge(vh_done, 4 * i + j + 1)
                sp.wait_ge(vl_done, 4 * i + j + 1)
                load_v(j, i + 1)
            sp.wait_ge(a_done, 4 * i + 4)
            load_d(i + 1)
        sp.wait_ge(wl_done, FRONT + N_U)
        sp.wait_ge(wh_done, FRONT + N_U)
        sp.dma_start(gfb[:, :], gfin).then_inc(gfin_in, 16)
        for q in range(2 * TT):
            tt, cols = q // 2, slice(q % 2 * 512, q % 2 * 512 + 512)
            sp.wait_ge(fin_done, q + 1)
            sp.dma_start(out[tt * P:(tt + 1) * P, cols], res[:, tt, cols]).then_inc(out_done, 16)
        sp.wait_ge(out_done, 16 * 2 * TT)

    @block.tensor
    def _(pe):
        def three(bank, lhs, rhs, first, last):
            (lh, ll), (rh, rl) = lhs, rhs
            pe.matmul(bank, lh, rh, start=first, stop=False)
            pe.matmul(bank, lh, rl, start=False, stop=False)
            return pe.matmul(bank, ll, rh, start=False, stop=last)

        def cols(j, split, free, h_ready=None, chunks=range(DC)):
            pe.wait_ge(wl_done, split)
            if free is not None:
                pe.wait_ge(bank_free, free)
            for c in chunks:
                if h_ready is not None and c == 0:
                    pe.wait_ge(hl_done, h_ready)
                if h_ready is not None and c == 4:
                    pe.wait_ge(hl2_done, TT if h_ready == TT else 2 * TT)
                mm = three(psum[:, j, :], (wH[:, j, c, :], wL[:, j, c, :]), (hH[:, c, :], hL[:, c, :]), c == 0, c == DC - 1)
            if c == DC - 1:
                mm.then_inc(bank_done, 1)

        def rows(g, tokens_first=False):
            order = [(tt, c) for tt in range(TT) for c in range(DC)] if tokens_first else \
                    [(tt, c) for j in range(4) for tt in range(TT) for c in (2 * j, 2 * j + 1)]
            for tt, c in order:
                j, part, tok = c // 2, slice(c % 2 * 4, c % 2 * 4 + 4), slice(tt * P, (tt + 1) * P)
                if tt == 0 and c % 2 == 0:
                    pe.wait_ge(wl_done, 4 * g + j + 1)
                if c == 0:
                    pe.wait_ge(bank_free, 4 * g + tt - 3)
                if g == WOUT and tt == 0:
                    pe.wait_ge(hl_done, TT + c + 1)
                mm = three(psum[:, tt, :], (hH[:, c, tok], hL[:, c, tok]), (wH[:, j, part, :], wL[:, j, part, :]), c == 0, c == DC - 1)
                if tt == TT - 1 and c % 2:
                    mm.then_inc(bank_done, 1)
                elif c == DC - 1:
                    mm.then_inc(rows_done, 1)
                if tokens_first and c == DC - 1 and tt:
                    norm_transposes("HT", 1, tt - 1)

        def side_bank(m):
            if m >= 4:
                pe.wait_ge(*evacuated(m - 4))
            return side(m)

        def norm_transposes(name, ph, tt):
            pe.wait_ge(diag_done, 4 * ph + tt + 1)
            for part in range(2):
                b = side_bank(side_at(name, 2 * tt + part))
                for q in range(4):
                    c = 4 * part + q
                    mm = pe.matmul(b[:, q * P:(q + 1) * P], res[:, tt, c * P:(c + 1) * P], rdiag[:, tt, :], start=True, stop=True)
                mm.then_inc(side_done, 1)

        def hh(h):
            return slice(h % 2 * 64, h % 2 * 64 + 64)

        def scores(c):
            b = side_bank(side_at("S", c))
            if c == 0:
                for q in range(4):
                    pe.wait_ge(*evacuated(side_at("QKT", q)))
            for h in range(H):
                mm = pe.matmul(b[:, h * P:(h + 1) * P], kT[:, h // 2, c * P:(c + 1) * P],
                               qz[:, h, c * P:(c + 1) * P], start=True, stop=True)
            mm.then_inc(side_done, 1)

        def chunk(c):
            b = side_bank(side_at("O", c))
            pe.wait_ge(*evacuated(side_at("S", c)))
            if c:
                pe.wait_ge(*evacuated(side_at("ST", c - 1)))
            for h in range(H):
                o = b[:, h * P:(h + 1) * P]
                mm = pe.matmul(o, scm[:, c % 2, h * P:(h + 1) * P], vt[:, c, h * P:(h + 1) * P], start=True, stop=(c == 0))
                if c:
                    mm = pe.matmul(o, qdz[:, h, c * P:(c + 1) * P], stat[:, (c - 1) % 2, h // 2, :],
                                   start=False, stop=True)
            mm.then_inc(side_done, 1)
            if c < TT - 1:
                b = side_bank(side_at("ST", c))
                pe.wait_ge(kd_done, 1)
                for h in range(H):
                    mm = pe.matmul(b[hh(h), h // 2 * P:(h // 2 + 1) * P], kd[:, c, h * 64:(h + 1) * 64],
                                   vt[:, c, h * P:(h + 1) * P], start=True, stop=True)
                mm.then_inc(side_done, 1)

        def tile(n, h_ready=None, chunks=range(DC)):
            cols(n % 4, n + 1, n - 3 if n >= 4 else None, h_ready, chunks)

        for tt in range(TT):
            norm_transposes("XT", 0, tt)
        for n in range(4 * UVAL, 4 * UGATE + 4):
            tile(n, TT if n == 0 else None)
        rows(QK)
        rows(VV)
        for n in range(4 * GRET, 4 * GRET + 4):
            tile(n)
            if n == 4 * GRET + 1:
                pe.wait_ge(rot_done, TT)
                for b in range(4):
                    bank = side_bank(side_at("QKT", b))
                    for tt in range(TT):
                        mm = pe.transpose(bank[:, tt * P:(tt + 1) * P], qkrot[:, tt, b * P:(b + 1) * P], ident)
                    mm.then_inc(side_done, 1)
        scores(0)
        pe.wait_ge(qd_done, H)
        for c in range(TT):
            tile(4 * GATE_A + c)
            chunk(c)
            if c < TT - 1:
                scores(c + 1)
        for n in range(4 * GATE_A + 4, 4 * GATE_A + 8):
            tile(n)
        for n in range(4 * GATE_B, 4 * GATE_B + 4):
            tile(n)
            if n == 4 * GATE_B:
                pe.wait_ge(y_done, TT)
                for h in range(H):
                    b = side_bank(side_at("YT", h))
                    for tt in range(TT):
                        mm = pe.transpose(b[:, tt * P:(tt + 1) * P], osb[:, tt, h * P:(h + 1) * P], ident)
                    mm.then_inc(side_done, 1)

        def channel_mean(name, src):
            b = side_bank(side_at(name))
            for ch in range(CH):
                mm = pe.matmul(b, ones, src[:, ch, :], start=(ch == 0), stop=(ch == CH - 1))
            mm.then_inc(side_done, 1)

        pe.wait_ge(conv_step, TAPS * CH)
        channel_mean("MU", cacc)
        for n in range(4 * GATE_B + 4, 4 * GATE_B + 8):
            tile(n)
            if n == 4 * GATE_B + 5:
                pe.wait_ge(sqc_done, CH)
                channel_mean("VAR", sqc)
        for i in range(DC):
            n = 4 * PROJ + i
            pe.wait_ge(wl_done, n + 1)
            pe.wait_ge(bank_free, n - 3)
            b = side_bank(side_at("PB", i))
            for c in range(DC):
                if i == 0:
                    pe.wait_ge(yl_done, c + 1)
                mm = three(stream(n) if c < 4 else b, (wH[:, n % 4, c, :], wL[:, n % 4, c, :]), (yH[:, c, :], yL[:, c, :]),
                           c % 4 == 0, c % 4 == 3)
                if c == 3:
                    mm.then_inc(side_done, 1)
            mm.then_inc(bank_done, 1)
        rows(WOUT)
        rows(WOUT + 1, tokens_first=True)
        norm_transposes("HT", 1, TT - 1)

        def query_scores(hp):
            b = side_bank(side_at("SC", hp))
            if hp == 0:
                pe.wait_ge(key_in, 16)
            pe.wait_ge(bank_free, 4 * QUERY + hp + 1)
            for tt in range(TT):
                mm = pe.matmul(b[:, tt * P:(tt + 1) * P], qT[:, hp, tt * P:(tt + 1) * P], keyT[:, hp, :], start=True, stop=True)
            mm.then_inc(side_done, 1)

        for hp in range(HP):
            tile(4 * QUERY + hp, 2 * TT + DC if hp == 0 else None)
            if hp:
                query_scores(hp - 1)
        for n in range(FRONT, MID):
            tile(n)
            if n == FRONT:
                query_scores(HP - 1)

        banks = [side_bank(side_at("ET", tt)) for tt in range(TT)]
        for w in range(2):
            for k in range(TOPK):
                pe.wait_ge(prod_done, w * TOPK + k + 2)
                for tt in range(TT):
                    pe.matmul(banks[tt][:, w * P:(w + 1) * P], prod[:, w, k, tt * P:(tt + 1) * P], identb[:, :], start=(k == 0), stop=(k == TOPK - 1))
        pe.wait_ge(pick_done, 1)
        for tt in range(TT):
            pe.transpose(banks[tt][:, 2 * P:3 * P], gtf[:, tt, :], ident).then_inc(side_done, 1)

        def half_tile(q):
            tile(MID + q // 2, chunks=range(q % 2 * 4, q % 2 * 4 + 4))

        half_tile(0)
        for part in range(2 * SEGMENTS):
            with pe.Fori(SEG2 * part, SEG2 * (part + 1)) as blk:
                for k in range(PER_BLK):
                    m = GATE0 + k
                    s, v = evacuated(m - 4)
                    pe.wait_ge(s, v + blk * (PER_BLK // 4))
                    pe.wait_ge(ohg_done, blk * PER_BLK + k + 1)
                    pe.wait_ge(ohx_done, blk * PER_BLK + k + 1)
                    for q in range(BATCH):
                        mm = pe.matmul(side(m)[:, q * P:(q + 1) * P], oh[:, k % 4, 0, q, :], oh[:, k % 4, 1, q, :], start=True, stop=True)
                    mm.then_inc(side_done, 1)
            if part + 1 < 2 * (SEGMENTS - 1):
                half_tile(part + 1)
        tile(MID + SEGMENTS - 1)

        def second(i, ops):
            v_hi, v_lo, a_hi, a_lo = ops
            for q in range(2 * TT):
                m = OUT0 + q
                s, v = evacuated(m - 4)
                pe.wait_ge(s, v + i * 2)
                tok, half = slice(q // 2 * P, (q // 2 + 1) * P), slice(q % 2 * 512, q % 2 * 512 + 512)
                for j in range(4):
                    if q == 0:
                        pe.wait_ge(vl_done, i * 4 + j + 1)
                        pe.wait_ge(al_done, i * 4 + j + 1)
                    mm = three(side(m), (a_hi[:, j, tok], a_lo[:, j, tok]), (v_hi[:, j, half], v_lo[:, j, half]), j == 0, j == 3)
                mm.then_inc(side_done, 1)

        with pe.Fori(0, LAST) as i:
            for j in range(4):
                n = FRONT + 4 * AHEAD + j
                cols(j, i * 4 + n + 1, i * 4 + n - 3)
            second(i, operands(None))
        with pe.Fori(0, AHEAD // 2) as i2:
            for k in range(2):
                second(i2 * 2 + LAST + k, operands(LAST + k))

    @block.scalar
    def _(act):
        def norm_square(ph, tt):
            if ph == 0:
                act.wait_ge(x_in[tt], 16)
            else:
                act.wait_ge(bank_free, 4 * WOUT + 4 + tt + 1)
            if ph or tt:
                act.wait_ge(sq_done, 4 * ph + tt)
            act.activation(junk[:, :], res[:, tt, :], ACT.Square, accum_out=ssq[:, tt:tt + 1]).then_inc(sq_done, 1)

        def norm_root(ph, tt):
            act.wait_ge(ms_done, 5 * ph + tt + 1)
            act.activation(rst[:, tt:tt + 1], rst[:, tt:tt + 1], ACT.Sqrt).then_inc(rt_done, 1)

        def norm_hi(name, tt):
            for part in range(2):
                act.wait_ge(*evacuated(side_at(name, 2 * tt + part)))
                act.activation(*(buf[:, 4 * part:4 * part + 4, tt * P:(tt + 1) * P] for buf in (hH, hraw)), ACT.Copy).then_inc(hh_done, 1)

        def w_hi(j, landed, freed):
            act.wait_ge(w_in[j], landed)
            if freed is not None:
                act.wait_ge(bank_done, freed)
            act.activation(wH[:, j, :, :], wraw[:, j, :, :], ACT.Copy).then_inc(wh_done, 1)

        def w_hi_tile(n):
            w_hi(n % 4, 16 * (n // 4 + 1), n - 3 if n >= 4 else None)

        def copy_out(n, dst, func=ACT.Copy):
            act.wait_ge(*bank_ready(n))
            act.activation(dst, stream(n), func).then_inc(bank_free, 1)

        def side_out(m, dst):
            act.wait_ge(side_done, m + 1)
            act.activation(dst, side(m), ACT.Copy).then_inc(side_free[m % 4], 1)

        def score_out(hp):
            if hp >= 8:
                act.wait_ge(topk_head, hp // 2 - 3)
            side_out(side_at("SC", hp), sc[:, hp // 2 % 4, hp % 2, :, :].rearrange("p t n -> p (t n)"))

        act.wait_ge(ones_done, 1)
        act.activation(rst, rst, ACT.Sqrt).then_inc(act_step, 1)
        for tt in range(TT):
            norm_square(0, tt)
            norm_root(0, tt)
        norm_hi("XT", 0)
        w_hi_tile(0)
        for tt in range(1, TT):
            norm_hi("XT", tt)
        w_hi_tile(1)
        nxt = 2
        for n in range(MID):
            g, j = n // 4, n % 4
            used = (4 * g if j < 3 else n) if g == WOUT + 1 else 4 * g + 3 if g in ROWS else n
            while nxt - 4 < used:
                w_hi_tile(nxt)
                nxt += 1
            if g == UVAL:
                copy_out(n, val[:, j, :])
            elif g == UGATE:
                copy_out(n, sg[:, j, :], ACT.Sigmoid)
            elif g == QK:
                copy_out(n, qkraw[:, j, :])
            elif g == VV:
                copy_out(n, vt[:, j, :])
            elif g == GRET:
                copy_out(n, gs[:, j, :], ACT.Silu)
            elif g in (GATE_A, GATE_A + 1):
                copy_out(n, sa[:, n - 4 * GATE_A, :], ACT.Sigmoid)
            elif g in (GATE_B, GATE_B + 1):
                copy_out(n, sb[:, n - 4 * GATE_B, :], ACT.Sigmoid)
            elif g in (PROJ, PROJ + 1):
                i = n - 4 * PROJ
                act.wait_ge(mix_done, i + 1)
                act.activation(hH[:, i, :], sa[:, i, :], ACT.Copy).then_inc(hh_done, 1)
            elif QUERY <= g < EXPERTS:
                hp = n - 4 * QUERY
                copy_out(n, qT[:, hp, :])
                if hp:
                    score_out(hp - 1)
            elif g >= EXPERTS:
                u = n - FRONT
                copy_out(n, gel[:, (u // 4 + 1) % 4, j, :], ACT.Gelu)
                if u == 0:
                    score_out(HP - 1)
                if u == 6:
                    act.wait_ge(exp_in, 1)
                    act.activation(best[:, :, :, :].rearrange("p a b c -> p (a b c)"), dec[:, 3, :], ACT.Exp).then_inc(exp_done, 1)
            if n == 4 * GRET + 2:
                for b in range(2):
                    m = side_at("QKT", b)
                    act.wait_ge(side_done, m + 1)
                    act.activation(qz[:, 2 * b, :], side(m), ACT.Copy, scale=C("half")[:, 0:1])
                    act.activation(qz[:, 2 * b + 1, :], side(m), ACT.Copy, scale=C("half")[:, 1:2]).then_inc(side_free[m % 4], 1)
                for b in range(2):
                    side_out(side_at("QKT", 2 + b), kT[:, b, :])
            if g == GATE_A:
                side_out(side_at("O", j), osb[:, j, :])
            if n == 4 * GATE_A + 5:
                act.wait_ge(ms_done, TT + 1)
                act.activation(grs, grs, ACT.Sqrt).then_inc(rt_done, 1)
            if n == 4 * GATE_B + 1:
                for h in range(H):
                    act.wait_ge(*evacuated(side_at("YT", h)))
                    act.activation(yH[:, h, :], gs[:, h, :], ACT.Copy).then_inc(yh_done, 1)
            if n == 4 * GATE_B + 4:
                for ch in range(CH):
                    act.wait_ge(cen_done, ch + 1)
                    act.activation(sqc[:, ch, :], cacc[:, ch, :], ACT.Square).then_inc(sqc_done, 1)
            if n == 4 * GATE_B + 5:
                act.wait_ge(*evacuated(side_at("VAR")))
                act.activation(rsd[:, :], rsd[:, :], ACT.Sqrt).then_inc(rt_done, 1)
            if n == 4 * GATE_B + 6:
                for ch in range(CH):
                    act.wait_ge(cn_done, ch + 1)
                    act.activation(sqc[:, ch, :], cacc[:, ch, :], ACT.Silu, bias=PR("ln_b", ch), scale=PR("ln_g", ch)).then_inc(yc_done, 1)
                for ch in range(CH):
                    act.wait_ge(yc_done, ch + 1)
                    act.activation(yH[:, 4 + ch, :], sqc[:, ch, :], ACT.Copy).then_inc(yh_done, 1)
            if g == WOUT + 1:
                norm_square(1, j)
                norm_root(1, j)
                if j:
                    norm_hi("HT", j - 1)
                if j == TT - 1:
                    norm_hi("HT", j)

        for tt in range(TT):
            m = side_at("ET", tt)
            act.wait_ge(side_done, m + 1)
            act.activation(eT[:, tt * NB:(tt + 1) * NB, :, :].rearrange("p n q b -> p q n b"),
                           side(m)[:, 0:3 * P].rearrange("p (q n b) -> p q n b", q=3, b=BATCH),
                           ACT.Copy).then_inc(side_free[m % 4], 1)

        act.wait_ge(bank_free, MID)
        act.activation(iota_psum, iota, ACT.Copy).then_inc(iota_done, 1)

        def distance(b, k, first=False):
            if not first:
                wait_now(act, "act", ohx_done, b + k - 1)
            act.activation(dist[:, k % 2, :], iota, ACT.Abs, scale=-1.0, bias=flat_eT[:, bass.ds((b + k) * (3 * BATCH), 1)]).then_inc(dist_done, 1)

        def one_hot(b, k):
            act.wait_ge(dist_done, b + k + 1)
            act.activation(oh[:, k % 4, 0, 0, :], dist[:, k % 2, :], ACT.Relu, scale=-1.0, bias=1.0).then_inc(ohx_done, 1)

        def stage_block(s, b2, first, last=False):
            if not first:
                act.wait_ge(stored[s], b2 * 16)
            for k in range(PER_BLK):
                m, b = GATE0 + s * PER_BLK + k, b2 * (2 * PER_BLK) + s * PER_BLK
                ahead = not last or k + 3 < PER_BLK
                if ahead:
                    distance(b, k + 3)
                act.wait_ge(side_done, b2 * (2 * PER_BLK) + m + 1)
                act.activation(stage[:, s, :, k * BATCH:(k + 1) * BATCH].rearrange("p e t -> p t e"),
                               side(m).rearrange("p (t e) -> p t e", t=BATCH), ACT.Copy).then_inc(side_free[m % 4], 1)
                if ahead:
                    one_hot(b, k + 3)

        for tt in range(TT):
            act.wait_ge(*evacuated(side_at("ET", tt)))
        for k in range(3):
            distance(0, k, first=(k < 2))
            one_hot(0, k)
        w_hi_tile(MID + 3)
        for seg in range(SEGMENTS):
            if seg == 0:
                for b2 in range(SEG2):
                    for s in range(2):
                        stage_block(s, b2, b2 == 0)
            else:
                with act.Fori(SEG2 * seg, SEG2 * (seg + 1) - (seg == SEGMENTS - 1)) as b2:
                    for s in range(2):
                        stage_block(s, b2, False)
            if seg == SEGMENTS - 1:
                for s in range(2):
                    stage_block(s, NBLK // 2 - 1, False, last=(s == 1))
            copy_out(MID + seg, gel[:, 0, seg, :], ACT.Gelu)
            if seg < SEGMENTS - 1:
                w_hi_tile(MID + 4 + seg)

        def group(i, k, ops, free, first_prod=True, w_ahead=4):
            def v_hi(j):
                act.wait_ge(v_in[j], i * 16 + 16)
                act.wait_ge(*free)
                act.activation(ops[0][:, j, :], vraw[:, j, :], ACT.Copy).then_inc(vh_done, 1)

            v_hi(0)
            for j in range(4):
                n = FRONT + 4 * AHEAD + j
                if j < w_ahead:
                    w_hi((n + 3) % 4, i * 16 + 16 * ((n + 3) // 4 + 1), i * 4 + n)
                if j < 3:
                    v_hi(j + 1)
                act.wait_ge(a_done, i * 4 + j + 1)
                act.activation(ops[2][:, j, :], gel[:, (k + 1) % 4, j, :], ACT.Copy).then_inc(ah_done, 1)
                if first_prod:
                    act.wait_ge(bank_done, i * 4 + n + 1)
                    act.wait_ge(al_done, i * 4 + j + 1)
                    act.activation(gel[:, (k + AHEAD + 1) % 4, j, :], psum[:, j, :], ACT.Gelu).then_inc(bank_free, 1)

        for s in stored:
            act.wait_ge(s, 16 * NBLK // 2)
        for i in range(4):
            group(i, i, operands(None), (side_done, OUT0 + 8 * i))
        with act.Fori(1, LAST // 4 - 1) as i4:
            for k in range(4):
                group(i4 * 4 + k, k, operands(None), (side_done, i4 * 32 + OUT0 + 8 * k))
        for i in range(LAST - 4, LAST):
            group(i, i % 4, operands(None), (side_done, OUT0 + 8 * i), w_ahead=min(4, N_U - 4 * (i + AHEAD) - 3))
        for i in range(LAST, GROUPS):
            free = (bank_done, FRONT + N_U) if i == LAST else (side_done, OUT0 + 8 * (i - 1))
            group(i, i % 4, operands(i), free, first_prod=False, w_ahead=0)

        for tt in range(TT):
            for half in range(2):
                act.wait_ge(*evacuated(OUT0 + 8 * (GROUPS - 1) + 2 * tt + half))
            act.wait_ge(sq_done, 8 + tt)
            act.activation(fjunk[:, :], res[:, tt, :], ACT.Square, accum_out=ssq[:, tt:tt + 1]).then_inc(sq_done, 1)
            act.wait_ge(ms_done, 2 * TT + 1 + tt + 1)
            act.activation(rst[:, tt:tt + 1], rst[:, tt:tt + 1], ACT.Sqrt).then_inc(rt_done, 1)

    @block.gpsimd
    def _(pool):
        steps = [0]

        def step(ins):
            ins.then_inc(pool_step, 1)
            steps[0] += 1
            return steps[0]

        def w_lo(j, count):
            pool.wait_ge(wh_done, count)
            pool.tensor_tensor(wL[:, j, :, :], wraw[:, j, :, :], f(wH[:, j, :, :]), ALU.subtract).then_inc(wl_done, 1)

        def rotate(tt):
            pool.wait_ge(bank_free, 4 * QK + tt + 1)
            v = qkraw[:, tt, :].rearrange("p (s h f i) -> p s h f i", s=2, h=H, f=2)
            o = qkrot[:, tt, :].rearrange("p (s h f i) -> p s h f i", s=2, h=H, f=2)
            r = [rtmp[:, q, :].rearrange("p (s h i) -> p s h i", s=2, h=H) for q in range(4)]
            cs, sn = (bc(tab[:, tt, :, :], 2, H) for tab in (cosv, sinv))
            if tt:
                pool.wait_ge(pool_step, 5 * tt)
                pool.wait_ge(rot_done, tt)
            step(pool.tensor_tensor(r[0], v[:, :, :, 0, :], cs, ALU.mult))
            n1 = step(pool.tensor_tensor(r[1], v[:, :, :, 1, :], sn, ALU.mult))
            step(pool.tensor_tensor(r[2], v[:, :, :, 0, :], sn, ALU.mult))
            n2 = step(pool.tensor_tensor(r[3], v[:, :, :, 1, :], cs, ALU.mult))
            pool.wait_ge(pool_step, n1)
            pool.wait_ge(pool_step, n2)
            step(pool.tensor_tensor(o[:, :, :, 0, :], r[0], r[1], ALU.subtract))
            pool.tensor_tensor(o[:, :, :, 1, :], r[2], r[3], ALU.add).then_inc(rot_done, 1)

        def norm_lo(tt, hh0):
            pool.wait_ge(hh_done, hh0 + 2 * tt + 2)
            h, l, x = (buf[:, 4:DC, tt * P:(tt + 1) * P] for buf in (hH, hL, hraw))
            pool.tensor_tensor(l, x, f(h), ALU.subtract).then_inc(hl2_done, 1)

        pool.memset(rst, 1.0).then_inc(ones_done, 1)
        pool.memset(cpad[:, :, 0:TAPS - 1], 0.0).then_inc(pad_done, 1)
        norm_lo(0, 0)
        for n in range(MID + 3):
            w_lo(n % 4, n + 1)
            if n == 0:
                for tt in range(1, TT):
                    norm_lo(tt, 0)
            if n == 4 * WOUT + 7:
                norm_lo(0, 2 * DC)
                norm_lo(1, 2 * DC)
            if n == 4 * QUERY + 1:
                norm_lo(2, 2 * DC)
                norm_lo(3, 2 * DC)
            if n == 4 * VV + 3:
                pool.wait_ge(cst_in, 16)
            if 0 <= n - (4 * VV + 3) < TT:
                rotate(n - (4 * VV + 3))
            if n == 4 * GRET + 3:
                pool.wait_ge(rot_done, TT)
                pool.tensor_tensor(kd[:, :, :].rearrange("p t (h d) -> p t h d", h=H),
                                   qkrot[:, :, 256:512].rearrange("p t (h d) -> p t h d", h=H),
                                   bc(bc(C("kdec"), 1, TT), 3, 64), ALU.mult).then_inc(kd_done, 1)
        for tt in range(TT):
            pool.wait_ge(*evacuated(side_at("ET", tt)))
        for seg in range(SEGMENTS):
            with pool.Fori(2 * SEG2 * seg, 2 * SEG2 * (seg + 1)) as blk:
                for k in range(PER_BLK):
                    gates = flat_eT[:, bass.ds((blk * PER_BLK + k) * (3 * BATCH) + 2 * BATCH, BATCH)]
                    wait_now(pool, "pool", oh_done, blk * PER_BLK + k + 1)
                    pool.tensor_tensor(oh[:, k % 4, 1, :, :], oh[:, k % 4, 1, :, :], bc(gates, 2, P), ALU.mult).then_inc(ohg_done, 1)
            if seg == 0:
                w_lo((MID + 3) % 4, MID + 4)
        for n in range(MID + 4, MID + 7):
            w_lo(n % 4, n + 1)
        with pool.Fori(0, (N_U - 4 * AHEAD - 4) // 4) as i:
            for j in range(4):
                n = FRONT + 4 * AHEAD + 3 + j
                w_lo(n % 4, i * 4 + n + 1)
        w_lo((FRONT + N_U - 1) % 4, FRONT + N_U)

    @block.vector
    def _(dve):
        steps = [0]

        def step(ins):
            ins.then_inc(dve_step, 1)
            steps[0] += 1
            return steps[0]

        def norm(name, ph, gain, hh0, before=None):
            def raw(tt, part):
                m = side_at(name, 2 * tt + part)
                dve.wait_ge(side_done, m + 1)
                a = PARAM_AT[gain][0] + 4 * part
                dve.tensor_tensor(hraw[:, 4 * part:4 * part + 4, tt * P:(tt + 1) * P], side(m).rearrange("p (c t) -> p c t", c=4),
                                  bc(prm[:, a:a + 4], 2, P), ALU.mult).then_inc(side_free[m % 4], 1)

            def lo(tt):
                dve.wait_ge(hh_done, hh0 + 2 * tt + 1)
                h, l, x = (buf[:, 0:4, tt * P:(tt + 1) * P] for buf in (hH, hL, hraw))
                dve.tensor_tensor(l, x, f(h), ALU.subtract).then_inc(hl_done, 1)

            for tt in range(TT):
                one = rst[:, tt:tt + 1]
                if before:
                    before(tt)
                    if tt:
                        raw(tt - 1, 0)
                dve.wait_ge(sq_done, 4 * ph + tt + 1)
                dve.tensor_scalar(one, ssq[:, tt:tt + 1], 1.0 / D, RMS_EPS, ALU.mult, ALU.add).then_inc(ms_done, 1)
                if before and tt:
                    raw(tt - 1, 1)
                dve.wait_ge(rt_done, 6 * ph + tt + 1)
                dve.wait_ge(dve_step, step(dve.reciprocal(one, one)))
                dve.tensor_scalar(rdiag[:, tt, :], ident, one, None, ALU.mult).then_inc(diag_done, 1)
                if tt:
                    if not before:
                        raw(tt - 1, 0)
                        raw(tt - 1, 1)
                    else:
                        lo(tt - 1)
            if not before:
                for tt in range(TT - 2):
                    lo(tt)
            raw(TT - 1, 0)
            raw(TT - 1, 1)
            if not before:
                lo(TT - 2)
            lo(TT - 1)

        def tap(k):
            for ch in range(CH):
                dve.wait_ge(conv_step, k * CH + ch - CH + 1)
                dve.scalar_tensor_tensor(cacc[:, ch, :], cpad[:, ch, bass.ds(k, T)],
                                         prm[:, bass.ds(k + PARAM_AT["dww"][0] + ch * TAPS, 1)],
                                         cacc[:, ch, :], ALU.mult, ALU.add).then_inc(conv_step, 1)

        def mask(c):
            m = side_at("S", c)
            dve.wait_ge(side_done, m + 1)
            dve.tensor_tensor(scm[:, c % 2, :], side(m), C("mask"), ALU.mult).then_inc(side_free[m % 4], 1)

        def next_state(c):
            m = side_at("ST", c)
            dve.wait_ge(side_done, m + 1)
            for b in range(2):
                src, dst = side(m)[:, b * P:(b + 1) * P], stat[:, c % 2, b, :]
                if c == 0:
                    ins = dve.tensor_copy(dst, src)
                else:
                    if b == 0:
                        dve.wait_ge(state_done, c)
                    else:
                        dve.wait_ge(*evacuated(side_at("ST", c - 1)))
                    ins = dve.scalar_tensor_tensor(dst, stat[:, (c - 1) % 2, b, :], C("cdec")[:, b:b + 1], src, ALU.mult, ALU.add)
                ins.then_inc(state_done if b == 0 else side_free[m % 4], 1)

        dve.wait_ge(prm_in, 16)
        dve.wait_ge(id_in, 16)
        dve.wait_ge(act_step, 1)
        norm("XT", 0, "g_mix", 0)
        dve.wait_ge(pad_done, 1)
        for ch in range(CH):
            dve.wait_ge(bank_free, 4 * UGATE + ch + 1)
            dve.tensor_tensor(cpad[:, ch, TAPS - 1:], val[:, ch, :], sg[:, ch, :], ALU.mult).then_inc(conv_in, 1)
        for ch in range(CH):
            dve.wait_ge(conv_in, ch + 1)
            dve.tensor_scalar(cacc[:, ch, :], cpad[:, ch, 0:T], PR("dww", ch * TAPS), PR("dwb", ch), ALU.mult, ALU.add).then_inc(conv_step, 1)
        with dve.Fori(1, 20) as k:
            tap(k)
        for b in range(2):
            dve.wait_ge(*evacuated(side_at("QKT", b)))
            for h in (2 * b, 2 * b + 1):
                dve.tensor_tensor(qdz[:, h, :].rearrange("p (t n) -> p t n", t=TT), qz[:, h, :].rearrange("p (t n) -> p t n", t=TT),
                                  bc(C("qdec")[:, b * P:(b + 1) * P], 1, TT), ALU.mult).then_inc(qd_done, 1)
        mask(0)
        for c in range(TT - 1):
            tap(20 + 2 * c)
            next_state(c)
            mask(c + 1)
            tap(21 + 2 * c)
        for c in range(TT):
            dve.wait_ge(*evacuated(side_at("O", c)))
            for h in range(H):
                n0 = step(dve.bn_stats(bst[:, c * H + h, :], osb[:, c, h * P:(h + 1) * P]))
        for n in range(TT * H):
            dve.wait_ge(dve_step, n0 - TT * H + n + 1)
            last = step(dve.bn_aggr(mv[:, n, :], bst[:, n, :]))
        dve.wait_ge(dve_step, last)
        dve.tensor_scalar(grs, mv[:, :, 1], LN_EPS, None, ALU.add).then_inc(ms_done, 1)
        dve.wait_ge(rt_done, TT + 1)
        dve.wait_ge(dve_step, step(dve.reciprocal(grs, grs)))
        for c in range(TT):
            for h in range(H):
                o = osb[:, c, h * P:(h + 1) * P]
                ins = dve.tensor_scalar(o, o, mv[:, c * H + h, 0:1], grs[:, c * H + h:c * H + h + 1], ALU.subtract, ALU.mult)
            ins.then_inc(y_done, 1)
        with dve.Fori(26, TAPS) as k:
            tap(k)

        def y_lo(c, src):
            dve.wait_ge(yh_done, c + 1)
            dve.tensor_tensor(yL[:, c, :], src, f(yH[:, c, :]), ALU.subtract).then_inc(yl_done, 1)

        for h in range(H):
            m = side_at("YT", h)
            dve.wait_ge(side_done, m + 1)
            dve.scalar_tensor_tensor(gs[:, h, :], side(m), PR("gn", h), gs[:, h, :], ALU.mult, ALU.mult).then_inc(side_free[m % 4], 1)
        for h in range(H):
            y_lo(h, gs[:, h, :])
        m = side_at("MU")
        dve.wait_ge(side_done, m + 1)
        dve.tensor_copy(rsd[:, :], side(m)).then_inc(side_free[m % 4], 1)
        dve.wait_ge(*evacuated(m))
        for ch in range(CH):
            dve.tensor_tensor(cacc[:, ch, :], cacc[:, ch, :], rsd[:, :], ALU.subtract).then_inc(cen_done, 1)
        m = side_at("VAR")
        dve.wait_ge(side_done, m + 1)
        dve.tensor_scalar(rsd[:, :], side(m), LN_EPS, None, ALU.add).then_inc(side_free[m % 4], 1)
        dve.wait_ge(rt_done, TT + 2)
        dve.wait_ge(dve_step, step(dve.reciprocal(rsd[:, :], rsd[:, :])))
        for ch in range(CH):
            dve.tensor_tensor(cacc[:, ch, :], cacc[:, ch, :], rsd[:, :], ALU.mult).then_inc(cn_done, 1)
        for ch in range(CH):
            y_lo(4 + ch, sqc[:, ch, :])

        def mix_lo(i):
            dve.wait_ge(hh_done, DC + i + 1)
            dve.tensor_tensor(hL[:, i, :], sa[:, i, :], f(hH[:, i, :]), ALU.subtract).then_inc(hl_done, 1)

        dve.wait_ge(bank_free, 4 * PROJ)
        for i in range(DC):
            m, n = side_at("PB", i), 4 * PROJ + i
            dve.wait_ge(bank_done, n + 1)
            dve.scalar_tensor_tensor(tb[:, i % 2, :], side(m), PR("bproj", i), sb[:, i, :], ALU.add, ALU.mult).then_inc(side_free[m % 4], 1)
            dve.tensor_tensor(sa[:, i, :], stream(n), sa[:, i, :], ALU.mult).then_inc(bank_free, 1)
            dve.wait_ge(*evacuated(m))
            dve.wait_ge(bank_free, n + 1)
            dve.tensor_tensor(sa[:, i, :], sa[:, i, :], tb[:, i % 2, :], ALU.add).then_inc(mix_done, 1)
            if i:
                mix_lo(i - 1)
        mix_lo(DC - 1)

        def add_row(g, tt):
            n = 4 * (WOUT + g) + tt
            dve.wait_ge(*bank_ready(n))
            r = res[:, tt, g * 512:(g + 1) * 512]
            dve.tensor_tensor(r, r, stream(n), ALU.add).then_inc(bank_free, 1)

        for tt in range(TT):
            add_row(0, tt)
        norm("HT", 1, "g_ffn", 2 * DC, lambda tt: add_row(1, tt))

        N_STEPS = 68

        def top16(head, slot, t0, q):
            par = slot % 2
            units = [(p, tt) for p in range(2) for tt in range(TT)]
            for p in range(2):
                m = side_at("SC", 2 * slot + p)
                wait_now(dve, "dve", side_free[m % 4], q * 2 + m // 4 + 1)
                for tt in range(TT):
                    dve.max(s16[:, par, p, tt, 0:8], sc[:, slot, p, tt, :]).then_inc(topk, 1)

            def ready(u, n):
                if u % 4 == 0:
                    wait_now(dve, "dve", topk, n)

            for u, (p, tt) in enumerate(units):
                ready(u, t0 + u + 4)
                dve.max_index(ix[:, par, p, tt, 0:8], s16[:, par, p, tt, 0:8], sc[:, slot, p, tt, :]).then_inc(topk, 1)
            for u, (p, tt) in enumerate(units):
                ready(u, t0 + 8 + u + 4)
                dve.match_replace(sc[:, slot, p, tt, :], s16[:, par, p, tt, 0:8], sc[:, slot, p, tt, :], NEG).then_inc(topk, 1)
            for u, (p, tt) in enumerate(units):
                ready(u, t0 + 16 + u + 4)
                dve.max(s16[:, par, p, tt, 8:16], sc[:, slot, p, tt, :]).then_inc(topk, 1)
            for u, (p, tt) in enumerate(units):
                ready(u, t0 + 24 + u + 4)
                dve.max_index(ix[:, par, p, tt, 8:16], s16[:, par, p, tt, 8:16], sc[:, slot, p, tt, :])\
                   .then_inc(topk if u < 7 else topk_head, 1)
            for i0, (r0, r1, w) in enumerate(RECTS):
                at0 = sum((b - a) * c for a, b, c in RECTS[:i0])
                o = cand[:, par, :, at0:at0 + (r1 - r0) * w].rearrange("p t (i j) -> p t i j", j=w)
                dve.tensor_tensor(o, bc(s16[:, par, 0, :, r0:r1], 3, w), bc(s16[:, par, 1, :, 0:w], 2, r1 - r0), ALU.add).then_inc(topk, 1)
            wait_now(dve, "dve", topk, t0 + 36)
            if slot == 0:
                wait_now(dve, "dve", side_done, q * 8 + side_at("SC", 3) + 1)
            dve.tensor_copy(i1f[:, :, bass.ds(head, 1), :].rearrange("p t a k -> p t (a k)"), ix[:, par, 0, :, :]).then_inc(topk, 1)
            wait_now(dve, "dve", topk_head, head + 1)
            dve.tensor_copy(i2f[:, :, bass.ds(head, 1), :].rearrange("p t a k -> p t (a k)"), ix[:, par, 1, :, :]).then_inc(topk, 1)
            t1 = t0 + 46

            def picks(buf, tt, a):
                return buf[:, par, tt, a:a + 8]

            ready(0, t1)
            for tt in range(TT):
                dve.max(picks(b16, tt, 0), cand[:, par, tt, :]).then_inc(topk, 1)
            for tt in range(TT):
                ready(tt, t1 + 4)
                dve.max_index(picks(p16, tt, 0), picks(b16, tt, 0), cand[:, par, tt, :]).then_inc(topk, 1)
            for tt in range(TT):
                ready(tt, t1 + 8)
                dve.match_replace(cand[:, par, tt, :], picks(b16, tt, 0), cand[:, par, tt, :], NEG).then_inc(topk, 1)
            for tt in range(TT):
                ready(tt, t1 + 12)
                dve.max(picks(b16, tt, 8), cand[:, par, tt, :]).then_inc(topk, 1)
            for tt in range(TT):
                ready(tt, t1 + 16)
                dve.max_index(picks(p16, tt, 8), picks(b16, tt, 8), cand[:, par, tt, :]).then_inc(topk, 1)
            for n, (dst, src) in enumerate(((best, b16), (pos, p16))):
                wait_now(dve, "dve", topk, t1 + 16 + 4 * n)
                dve.tensor_copy(dst[:, :, bass.ds(head, 1), :].rearrange("p t a k -> p t (a k)"), src[:, par, :, :]).then_inc(topk, 1)

        with dve.Fori(0, 2) as q:
            for slot in range(4):
                top16(q * 4 + slot, slot, (q * 4 + slot) * N_STEPS, q)

        dve.wait_ge(topk, HEADS * N_STEPS)
        flat = "p a b c -> p (a b c)"
        dve.tensor_tensor(dec[:, 3, :].rearrange("p (a b) -> p a b", b=TOPK), best[:, :, :, :].rearrange("p a b c -> p (a b) c"),
                          best[:, :, :, 0:1].rearrange("p a b c -> p (a b) c").to_broadcast([P, TT * HEADS, TOPK]),
                          ALU.subtract).then_inc(exp_in, 1)
        n_p = step(dve.tensor_copy(dec[:, 0, :], pos[:, :, :, :].rearrange(flat)))
        dve.wait_ge(dve_step, n_p)
        n_i = step(dve.tensor_scalar(irank[:, :], dec[:, 0, :], -46.0, 0.0, ALU.add, ALU.max))
        dve.wait_ge(dve_step, n_i)
        n_j = step(dve.tensor_tensor(jrank[:, :], dec[:, 0, :], irank[:, :], ALU.subtract))
        for q, (b, w) in enumerate([(16, 16), (24, 8), (29, 5), (34, 5), (37, 3), (40, 3), (43, 3), (46, 3)]):
            n_t = step(dve.tensor_scalar(dec[:, 1 + q % 2, :], dec[:, 0, :], float(b), float(-w), ALU.is_ge, ALU.mult))
            dve.wait_ge(dve_step, n_i)
            n_i = step(dve.scalar_tensor_tensor(irank[:, :], dec[:, 0, :], float(b), irank[:, :], ALU.is_ge, ALU.add))
            dve.wait_ge(dve_step, n_j)
            dve.wait_ge(dve_step, n_t)
            n_j = step(dve.tensor_tensor(jrank[:, :], jrank[:, :], dec[:, 1 + q % 2, :], ALU.add))
        dve.wait_ge(dve_step, n_j)

        dve.tensor_copy(identb[:, :], ident).then_inc(prod_done, 1)

        def split_ranks(w):
            rank, index = ((irank, i1f), (jrank, i2f))[w]
            for k in range(TOPK):
                dve.scalar_tensor_tensor(prod[:, w, k, :].rearrange("p (a b) -> p a b", b=TOPK), rank[:, :].rearrange("p (a b) -> p a b", b=TOPK),
                                         float(k), index[:, :, :, k:k + 1].rearrange("p a b c -> p (a b) c").to_broadcast([P, TT * HEADS, TOPK]),
                                         ALU.is_equal, ALU.mult).then_inc(prod_done, 1)

        split_ranks(0)
        dve.wait_ge(exp_done, 1)
        dve.wait_ge(dve_step, step(dve.tensor_reduce(zs, best[:, :, :, :].rearrange("p a b c -> p (a b) c"), AX.X, ALU.add)))
        dve.wait_ge(dve_step, step(dve.reciprocal(zs, zs)))
        dve.tensor_tensor(gtf[:, :, :].rearrange("p a (b c) -> p (a b) c", c=TOPK), best[:, :, :, :].rearrange("p a b c -> p (a b) c"),
                          bc(zs, 2, TOPK), ALU.mult).then_inc(pick_done, 1)
        split_ranks(1)

        for tt in range(TT):
            dve.wait_ge(*evacuated(side_at("ET", tt)))
        dve.wait_ge(iota_done, 1)
        with dve.Fori(0, NBLK) as blk:
            for k in range(PER_BLK):
                dve.wait_ge(side_done, blk * PER_BLK + GATE0 + k - 3)
                dve.tensor_tensor(oh[:, k % 4, :, :, :].rearrange("p w q e -> p (w q) e")[:, 1:, :], bc(iota_psum, 1, 2 * BATCH - 1),
                                  bc(flat_eT[:, bass.ds((blk * PER_BLK + k) * (3 * BATCH) + 1, 2 * BATCH - 1)], 2, P),
                                  ALU.is_equal).then_inc(oh_done, 1)

        def prepare(i, k, j, ops):
            def v_lo(j):
                dve.wait_ge(vh_done, i * 4 + j + 1)
                dve.tensor_tensor(ops[1][:, j, :], vraw[:, j, :], f(ops[0][:, j, :]), ALU.subtract).then_inc(vl_done, 1)

            if j == 0:
                v_lo(0)
                dve.wait_ge(d_in, i * 16 + 16)
            g = gel[:, (k + 1) % 4, j, :]
            dve.wait_ge(bank_free, i * 4 + FRONT + j + 1)
            dve.tensor_tensor(g.rearrange("p (b t) -> p b t", t=TBLK), g.rearrange("p (b t) -> p b t", t=TBLK), dg[:, :, j, :],
                              ALU.mult).then_inc(a_done, 1)
            if j < 3:
                v_lo(j + 1)
            dve.wait_ge(ah_done, i * 4 + j + 1)
            dve.tensor_tensor(ops[3][:, j, :], g, f(ops[2][:, j, :]), ALU.subtract).then_inc(al_done, 1)

        def final_norm(tt):
            one = rst[:, tt:tt + 1]
            dve.wait_ge(sq_done, 8 + tt + 1)
            dve.tensor_scalar(one, ssq[:, tt:tt + 1], 1.0 / D, RMS_EPS, ALU.mult, ALU.add).then_inc(ms_done, 1)
            dve.wait_ge(rt_done, 2 * TT + 2 + tt + 1)
            dve.wait_ge(dve_step, step(dve.reciprocal(one, one)))
            if tt == 0:
                dve.wait_ge(gfin_in, 16)
            for half in range(2):
                cols = slice(half * 512, half * 512 + 512)
                dve.scalar_tensor_tensor(res[:, tt, cols], res[:, tt, cols], one, gfb[:, cols], ALU.mult, ALU.mult).then_inc(fin_done, 1)

        def add(i, q):
            m = OUT0 + q
            dve.wait_ge(side_done, i * 8 + m + 1)
            r = res[:, q // 2, q % 2 * 512:q % 2 * 512 + 512]
            dve.tensor_tensor(r, r, side(m), ALU.add).then_inc(side_free[m % 4], 1)

        def group(i, k):
            for j in range(4):
                prepare(i, k, j, operands(None))
            for q in range(2 * TT):
                add(i, q)

        with dve.Fori(0, LAST // 4 - 1) as i4:
            for k in range(4):
                group(i4 * 4 + k, k)
        for i in range(LAST - 4, LAST - 1):
            group(i, i % 4)
        for j in range(4):
            prepare(LAST - 1, (LAST - 1) % 4, j, operands(None))
        for i in range(LAST - 1, GROUPS):
            for j in range(4):
                if i + 1 < GROUPS:
                    prepare(i + 1, (i + 1) % 4, j, operands(i + 1))
                add(i, 2 * j)
                add(i, 2 * j + 1)
                if i == GROUPS - 1 and j:
                    final_norm(j - 1)
        final_norm(TT - 1)

    ctx.close()


def constants():
    import numpy as np
    gamma = 1.0 - 2.0 ** (-5.0 - np.arange(H, dtype=np.float64))
    inv = (1.0 / (np.float32(10000.0) ** (np.arange(32, dtype=np.float32) / np.float32(32)))).astype(np.float32)
    ang = (np.arange(T, dtype=np.float32)[:, None] * inv[None, :]).astype(np.float64)
    scale = np.array([1.0, 64 ** -0.5])
    rope = lambda a: (a[:, None, :] * scale[None, :, None]).reshape(TT, P, 64).transpose(1, 0, 2).reshape(P, -1)
    n = np.arange(P, dtype=np.float64)
    diff = n[None, :] - n[:, None]
    mask = np.stack([np.where(diff >= 0, g ** np.maximum(diff, 0), 0.0) for g in gamma], 1)
    pair = np.repeat(gamma.reshape(2, 2).T, 64, axis=0)
    parts = {
        "ident": np.eye(P), "iota": np.tile(n, (P, 1)), "ones": np.full((P, P), 1.0 / 512),
        "cos": rope(np.cos(ang)), "sin": rope(np.sin(ang)), "mask": mask.reshape(P, -1),
        "qdec": (pair[:, :, None] ** (n + 1.0)).reshape(P, -1),
        "kdec": gamma[None, :] ** (P - 1.0 - n[:, None]), "cdec": pair ** P, "half": np.stack([n < 64, n >= 64], 1),
    }
    return np.concatenate([parts[name] for name, _ in CONSTS], axis=1).astype(np.float32)


def kernel(**inputs):
    import numpy as np
    import concourse.bacc as bacc
    from concourse.bass_utils import run_bass_kernel_spmd as run

    a = {k: np.asarray(v) for k, v in inputs.items()}

    def tiles(w):
        k, n = w.shape
        return w.reshape(k // P, P, n // P, P).transpose(2, 1, 0, 3).reshape(n // P, P, -1)

    def cols(v):
        return v.reshape(-1, P).T

    def row_tiles(w):
        return w.reshape(4, 2, P, -1, 512).transpose(3, 0, 2, 1, 4).reshape(-1, P, D)

    w_in = a["w_in"][0]
    qk, v, g_ret, u_val, u_gate, gates = np.split(w_in, [512, 1024, 1536, 2048, 2560], axis=1)
    proj = tiles(np.concatenate([a["w_ret_proj"][0], a["w_conv_proj"][0]], axis=0))
    params = [cols(a["rms_mix_g"][0]), cols(a["rms_ffn_g"][0]), cols(a["ret_gn_g"][0].reshape(-1)), cols(a["conv_ln_g"][0]),
              cols(a["conv_ln_b"][0]), cols(a["conv_dw_b"][0]), cols(a["b_conv_proj"][0]),
              a["conv_dw_w"][0].reshape(TAPS, CH, P).transpose(2, 1, 0).reshape(P, -1)]
    arrays = {
        "x": a["x"][0],
        "wfront": np.concatenate([tiles(u_val), tiles(u_gate), row_tiles(qk), row_tiles(v), tiles(g_ret), tiles(gates), proj,
                                  row_tiles(a["w_out"][0]), tiles(a["w_query"][0])], axis=0),
        "ut": a["peer_u"][0].reshape(P, NKEY, DC, P).transpose(1, 3, 2, 0).reshape(NKEY, P, D),
        "peer_v": a["peer_v"][0].reshape(P, NKEY, D),
        "keys": a["peer_sub_keys"][0].transpose(3, 0, 1, 2).reshape(P, -1),
        "consts": constants(),
        "params": np.concatenate(params, axis=1),
        "gfin": np.broadcast_to(a["rms_final_g"], (P, D)),
    }
    arrays = {k: np.ascontiguousarray(v) for k, v in arrays.items()}
    nc = bacc.Bacc("TRN2", target_bir_lowering=False, num_devices=1)
    args = [nc.dram_tensor(k, v.shape, F32, kind="ExternalInput").ap() for k, v in arrays.items()]
    out = nc.dram_tensor("out", (T, D), F32, kind="ExternalOutput").ap()
    build(nc, *args, out)
    r = run(nc, [arrays], core_ids=[0])
    return r.results[0]["out"].reshape(1, T, D)
```
